# Optimizing a Trainium2 kernel written in Bass

```python
import math, functools
import jax, jax.numpy as jnp
from jax import lax
import numpy as np

D_MODEL = 1024
BATCH = 1
SEQ = 512
DEPTH = 1
DEC_BATCH = 8
DEC_SEQ = 8
PAST_LEN = 2048
PAGE_SIZE = 128

N_HEADS_A = 8
HEAD_DIM_A = 64
ROT_DIM = HEAD_DIM_A // 4
ROPE_THETA = 500000.0
N_HEADS_IDX = 4
IDX_DIM = 64
IDX_W_SCALE = (N_HEADS_IDX * IDX_DIM) ** -0.5
TOPK_MAX = 256
Q_BLOCK = 128
N_HEADS_B = 4
KEY_DIM_B = 128
VAL_DIM_B = 128
CHUNK_B = 16
WIDTH_A = N_HEADS_A * HEAD_DIM_A
WIDTH_B = N_HEADS_B * VAL_DIM_B
KEYW_B = N_HEADS_B * KEY_DIM_B
D_FF = ((8 * D_MODEL // 3 + 127) // 128) * 128
EPS = 1e-6
IN_SIZES = (WIDTH_A, WIDTH_A, WIDTH_A, N_HEADS_IDX * IDX_DIM, IDX_DIM, N_HEADS_IDX, KEYW_B, KEYW_B, WIDTH_B, WIDTH_B, D_MODEL, D_MODEL)
IN_OFFSETS = tuple(int(o) for o in np.cumsum(IN_SIZES)[:-1])
N_IN = int(sum(IN_SIZES))

kernel_name = 'dsa_hgrn2_gated_macaron_step'

def rms_norm(x, g):
    xf = x.astype(jnp.float32)
    y = xf * lax.rsqrt(jnp.mean(xf * xf, axis=-1, keepdims=True) + EPS)
    return (y * g.astype(jnp.float32)).astype(x.dtype)

def swiglu(h, w_gate, w_up, w_down):
    return (jax.nn.silu(h @ w_gate) * (h @ w_up)) @ w_down

def rotary(x, pos):
    inv = ROPE_THETA ** (-jnp.arange(0, ROT_DIM, 2, dtype=jnp.float32) / ROT_DIM)
    ang = pos.astype(jnp.float32)[:, None] * inv[None, :]
    cos = jnp.cos(ang)[:, None, :]
    sin = jnp.sin(ang)[:, None, :]
    xr = x[..., :ROT_DIM].astype(jnp.float32)
    x1, x2 = xr[..., :ROT_DIM // 2], xr[..., ROT_DIM // 2:]
    rot = jnp.concatenate([x1 * cos - x2 * sin, x2 * cos + x1 * sin], axis=-1).astype(x.dtype)
    return jnp.concatenate([rot, x[..., ROT_DIM:]], axis=-1)

def gather_rows(src, idx):
    return jax.vmap(lambda s, i: s[i])(src, idx)

def indexed_sparse_attention(q, iq, iw, qpos, ik_all, kv_gather):
    L = ik_all.shape[1]
    n_sel = min(TOPK_MAX, L // 4)
    dots = jnp.einsum('bthd,bsd->bths', iq.astype(jnp.float32), ik_all.astype(jnp.float32))
    score = jnp.einsum('bths,bth->bts', jax.nn.relu(dots), iw.astype(jnp.float32) * IDX_W_SCALE)
    admissible = jnp.arange(L, dtype=jnp.int32)[None, :] <= qpos[:, None]
    score = jnp.where(admissible[None], score, -jnp.inf)
    _, idx = lax.top_k(score, n_sel)
    valid = idx <= qpos[None, :, None]
    k_sel, v_sel = kv_gather(idx)
    logits = jnp.einsum('bthd,btkhd->bthk', q.astype(jnp.float32), k_sel.astype(jnp.float32)) * (HEAD_DIM_A ** -0.5)
    logits = jnp.where(valid[:, :, None, :], logits, -jnp.inf)
    p = jax.nn.softmax(logits, axis=-1)
    return jnp.einsum('bthk,btkhd->bthd', p.astype(v_sel.dtype), v_sel)

def prompt_attention(q, k, v, iq, ik, iw, pos):
    B, T = q.shape[:2]
    nb = T // Q_BLOCK

    def blocks(a):
        return jnp.moveaxis(a.reshape((B, nb, Q_BLOCK) + a.shape[2:]), 1, 0)

    def kv_gather(idx):
        return gather_rows(k, idx), gather_rows(v, idx)

    def body(blk):
        qb, iqb, iwb, pb = blk
        return indexed_sparse_attention(qb, iqb, iwb, pb, ik, kv_gather)

    out = lax.map(body, (blocks(q), blocks(iq), blocks(iw), pos.reshape(nb, Q_BLOCK)))
    return jnp.moveaxis(out, 0, 1).reshape(B, T, N_HEADS_A, HEAD_DIM_A)

def sample_attention(layer, cache_k, cache_v, cache_idx_k, page_table, q, k, v, iq, ik, iw, pos):
    B, T = q.shape[:2]
    ik_past = cache_idx_k[layer, page_table].reshape(B, PAST_LEN, IDX_DIM)
    ik_all = jnp.concatenate([ik_past.astype(ik.dtype), ik], axis=1)

    def kv_gather(idx):
        is_past = idx < PAST_LEN
        pidx = jnp.minimum(idx, PAST_LEN - 1)
        phys = jax.vmap(lambda pt, i: pt[i])(page_table, pidx // PAGE_SIZE)
        off = pidx % PAGE_SIZE
        kp = cache_k[layer, phys, off].astype(k.dtype)
        vp = cache_v[layer, phys, off].astype(v.dtype)
        nidx = jnp.clip(idx - PAST_LEN, 0, T - 1)
        m = is_past[..., None, None]
        return jnp.where(m, kp, gather_rows(k, nidx)), jnp.where(m, vp, gather_rows(v, nidx))

    return indexed_sparse_attention(q, iq, iw, pos, ik_all, kv_gather)

def hgrn2_chunked(q, k, logf, v, s0):
    B, T, H, DK = q.shape
    DV = v.shape[-1]
    n_chunks = -(-T // CHUNK_B)
    pad = n_chunks * CHUNK_B - T

    def to_chunks(a):
        a = jnp.pad(a.astype(jnp.float32), ((0, 0), (0, pad), (0, 0), (0, 0)))
        return a.reshape(B, n_chunks, CHUNK_B, H, a.shape[-1]).transpose(1, 0, 3, 2, 4)

    causal = jnp.tril(jnp.ones((CHUNK_B, CHUNK_B), dtype=bool))[:, :, None]

    def step(S, chunk):
        qc, kc, gc, vc = chunk
        b = jnp.cumsum(gc, axis=2)
        diff = jnp.where(causal, b[:, :, :, None, :] - b[:, :, None, :, :], -jnp.inf)
        att = jnp.einsum('bhtk,bhsk,bhtsk->bhts', qc, kc, jnp.exp(diff))
        out = jnp.einsum('bhtk,bhkv->bhtv', qc * jnp.exp(b), S) + jnp.einsum('bhts,bhsv->bhtv', att, vc)
        b_last = b[:, :, -1:, :]
        S = jnp.exp(b_last[:, :, 0, :])[..., None] * S + jnp.einsum('bhsk,bhsv->bhkv', kc * jnp.exp(b_last - b), vc)
        return S, out

    S, out = lax.scan(step, s0.astype(jnp.float32), (to_chunks(q), to_chunks(k), to_chunks(logf), to_chunks(v)))
    out = out.transpose(1, 0, 3, 2, 4).reshape(B, n_chunks * CHUNK_B, H, DV)[:, :T]
    return out, S.astype(s0.dtype)

def mixer_block(h, pos, attend, s0, w_in, q_norm, k_norm, lb, o_norm, w_proj_attn, w_proj_hgrn, w_out):
    B, T, _ = h.shape
    (q, k, v, iq, ik, iw, hq, hf, hi, hg, ga, gb) = jnp.split(h @ w_in, IN_OFFSETS, axis=-1)
    q = rotary(rms_norm(q.reshape(B, T, N_HEADS_A, HEAD_DIM_A), q_norm), pos)
    k = rotary(rms_norm(k.reshape(B, T, N_HEADS_A, HEAD_DIM_A), k_norm), pos)
    v = v.reshape(B, T, N_HEADS_A, HEAD_DIM_A)
    iq = rotary(iq.reshape(B, T, N_HEADS_IDX, IDX_DIM), pos)
    ik = rotary(ik[:, :, None, :], pos)[:, :, 0, :]
    attn = attend(q, k, v, iq, ik, iw, pos).reshape(B, T, WIDTH_A)
    zf = hf.astype(jnp.float32)
    logf = jnp.log(lb + (1.0 - lb) * jax.nn.sigmoid(zf))
    kf = (1.0 - lb) * jax.nn.sigmoid(-zf)
    o, s_new = hgrn2_chunked(jax.nn.silu(hq).reshape(B, T, N_HEADS_B, KEY_DIM_B),
                             kf.reshape(B, T, N_HEADS_B, KEY_DIM_B),
                             logf.reshape(B, T, N_HEADS_B, KEY_DIM_B),
                             hi.reshape(B, T, N_HEADS_B, VAL_DIM_B), s0)
    o = rms_norm(o.astype(h.dtype), o_norm) * jax.nn.silu(hg.reshape(B, T, N_HEADS_B, VAL_DIM_B))
    merged = jax.nn.sigmoid(ga) * (attn @ w_proj_attn) + jax.nn.sigmoid(gb) * (o.reshape(B, T, WIDTH_B) @ w_proj_hgrn)
    return merged @ w_out, k, v, ik, s_new

def decoder_layer(x, pos, attend, s0, ffn1, mix, ffn2):
    x = x + 0.5 * swiglu(rms_norm(x, ffn1[0]), ffn1[1], ffn1[2], ffn1[3])
    y, k, v, ik, s_new = mixer_block(rms_norm(x, mix[0]), pos, attend, s0, *mix[1:])
    x = x + y
    x = x + 0.5 * swiglu(rms_norm(x, ffn2[0]), ffn2[1], ffn2[2], ffn2[3])
    return x, k, v, ik, s_new

def setup_inputs(seed: int = 0) -> dict:
    key = jax.random.key(seed)
    ks = jax.random.split(key, 26)
    n_pages = PAST_LEN // PAGE_SIZE
    n_pool = (DEC_BATCH * n_pages * 5) // 4

    def w(k, shape, fan_in):
        return jax.random.normal(k, shape, jnp.float32) * (fan_in ** -0.5)

    def gain(k, shape):
        return 1.0 + 0.02 * jax.random.normal(k, shape, jnp.float32)

    page_table = jax.random.permutation(ks[6], n_pool)[:DEC_BATCH * n_pages].reshape(DEC_BATCH, n_pages).astype(jnp.int32)
    return {
        'x_prompt': jax.random.normal(ks[0], (BATCH, SEQ, D_MODEL), jnp.float32),
        'x_sample': jax.random.normal(ks[1], (DEC_BATCH, DEC_SEQ, D_MODEL), jnp.float32),
        'cache_k': jax.random.normal(ks[2], (DEPTH, n_pool, PAGE_SIZE, N_HEADS_A, HEAD_DIM_A), jnp.float32),
        'cache_v': jax.random.normal(ks[3], (DEPTH, n_pool, PAGE_SIZE, N_HEADS_A, HEAD_DIM_A), jnp.float32),
        'cache_idx_k': jax.random.normal(ks[4], (DEPTH, n_pool, PAGE_SIZE, IDX_DIM), jnp.float32),
        'state_hgrn': 0.5 * jax.random.normal(ks[5], (DEPTH, DEC_BATCH, N_HEADS_B, KEY_DIM_B, VAL_DIM_B), jnp.float32),
        'page_table': page_table,
        'ffn1_norm': gain(ks[7], (DEPTH, D_MODEL)),
        'ffn1_w_gate': w(ks[8], (DEPTH, D_MODEL, D_FF), D_MODEL),
        'ffn1_w_up': w(ks[9], (DEPTH, D_MODEL, D_FF), D_MODEL),
        'ffn1_w_down': w(ks[10], (DEPTH, D_FF, D_MODEL), D_FF),
        'mix_norm': gain(ks[11], (DEPTH, D_MODEL)),
        'w_in': w(ks[12], (DEPTH, D_MODEL, N_IN), D_MODEL),
        'q_norm': gain(ks[13], (DEPTH, HEAD_DIM_A)),
        'k_norm': gain(ks[14], (DEPTH, HEAD_DIM_A)),
        'hgrn_lb': 0.5 * jax.random.normal(ks[15], (DEPTH + 1, KEYW_B), jnp.float32),
        'hgrn_o_norm': gain(ks[16], (DEPTH, VAL_DIM_B)),
        'w_proj_attn': w(ks[17], (DEPTH, WIDTH_A, D_MODEL), WIDTH_A),
        'w_proj_hgrn': w(ks[18], (DEPTH, WIDTH_B, D_MODEL), WIDTH_B),
        'w_out': w(ks[19], (DEPTH, D_MODEL, D_MODEL), D_MODEL),
        'ffn2_norm': gain(ks[20], (DEPTH, D_MODEL)),
        'ffn2_w_gate': w(ks[21], (DEPTH, D_MODEL, D_FF), D_MODEL),
        'ffn2_w_up': w(ks[22], (DEPTH, D_MODEL, D_FF), D_MODEL),
        'ffn2_w_down': w(ks[23], (DEPTH, D_FF, D_MODEL), D_FF),
    }

def reference(x_prompt, x_sample, cache_k, cache_v, cache_idx_k, state_hgrn, page_table,
              ffn1_norm, ffn1_w_gate, ffn1_w_up, ffn1_w_down, mix_norm, w_in, q_norm, k_norm,
              hgrn_lb, hgrn_o_norm, w_proj_attn, w_proj_hgrn, w_out,
              ffn2_norm, ffn2_w_gate, ffn2_w_up, ffn2_w_down):
    pos_p = jnp.arange(SEQ, dtype=jnp.int32)
    pos_s = PAST_LEN + jnp.arange(DEC_SEQ, dtype=jnp.int32)
    lb_all = jnp.cumsum(jax.nn.softmax(hgrn_lb.astype(jnp.float32), axis=0), axis=0)
    xp, xs = x_prompt, x_sample
    kp_l, vp_l, ikp_l, sp_l, ks_l, vs_l, iks_l, ss_l = [], [], [], [], [], [], [], []
    for l in range(DEPTH):
        ffn1 = (ffn1_norm[l], ffn1_w_gate[l], ffn1_w_up[l], ffn1_w_down[l])
        ffn2 = (ffn2_norm[l], ffn2_w_gate[l], ffn2_w_up[l], ffn2_w_down[l])
        mix = (mix_norm[l], w_in[l], q_norm[l], k_norm[l], lb_all[l], hgrn_o_norm[l],
               w_proj_attn[l], w_proj_hgrn[l], w_out[l])
        s0_p = jnp.zeros((xp.shape[0], N_HEADS_B, KEY_DIM_B, VAL_DIM_B), xp.dtype)
        xp, kp, vp, ikp, sp = decoder_layer(xp, pos_p, prompt_attention, s0_p, ffn1, mix, ffn2)
        attend_s = functools.partial(sample_attention, l, cache_k, cache_v, cache_idx_k, page_table)
        xs, ks, vs, iks, ss = decoder_layer(xs, pos_s, attend_s, state_hgrn[l], ffn1, mix, ffn2)
        kp_l.append(kp); vp_l.append(vp); ikp_l.append(ikp); sp_l.append(sp)
        ks_l.append(ks); vs_l.append(vs); iks_l.append(iks); ss_l.append(ss)
    return (xp, xs,
            jnp.stack(kp_l), jnp.stack(vp_l), jnp.stack(ikp_l), jnp.stack(sp_l),
            jnp.stack(ks_l), jnp.stack(vs_l), jnp.stack(iks_l), jnp.stack(ss_l))


_drawn_inputs = setup_inputs


def setup_inputs(seed=0):
    import zlib

    import numpy as np

    out = dict(_drawn_inputs(seed))
    spreads = {}
    factors = {'ffn1_norm': 5.269,
     'q_norm': 200.0,
     'k_norm': 24.887,
     'hgrn_o_norm': 63.139,
     'ffn2_norm': 23.469}
    for name, (base, spread) in spreads.items():
        noise = np.random.default_rng([zlib.crc32(name.encode()), seed]).standard_normal(out[name].shape)
        drawn = base * np.exp(spread * noise) if base else spread * noise
        out[name] = __import__('jax').numpy.asarray(drawn.astype(out[name].dtype))
    for name, factor in factors.items():
        out[name] = (out[name] * factor).astype(out[name].dtype)
    return out
```

```python
from contextlib import ExitStack

import numpy as np

import concourse.bass as bass
from concourse import mybir

F32 = mybir.dt.float32
F32R = mybir.dt.float32r
BF16 = mybir.dt.bfloat16
I32 = mybir.dt.int32
ALU = mybir.AluOpType
ACT = mybir.ActivationFunctionType
AX_X = mybir.AxisListType.X

P = 128
D = 1024
SEQ = 512
NB, NQ = 8, 8
NS = NB * NQ
T = NS + SEQ
HT = T // 2
PAST, PAGE = 2048, 128
NPG = PAST // PAGE
HA, DH = 8, 64
HI, DI = 4, 64
ROT = DH // 4
HR = ROT // 2
TOPK = 256
TOPK_P = min(TOPK, SEQ // 4)
TOPK_S = min(TOPK, (PAST + NQ) // 4)
HB, KD, VD = 4, 128, 128
FF = ((8 * D // 3 + 127) // 128) * 128
EPS = 1e-6
THETA = 500000.0
DC = D // P
HALF = FF // P // 2
IN_SIZES = (512, 512, 512, HI * DI, DI, HI, 512, 512, 512, 512, D, D)
IN_OFF = [0] + [int(o) for o in np.cumsum(IN_SIZES)]
OQ, OK_, OV, OIQ, OIK, OIW, OHQ, OHF, OHI, OHG, OGA, OGB = IN_OFF[:12]
NT = 1 + SEQ // P
TILE_AT = [0] + [NS + P * i for i in range(SEQ // P)]
IDX_SCALE = float((HI * DI) ** -0.5)
UNIT = 16 * P
NRAW, NW = 3, 2


def weight_units(w):
    def cols(name, rows, at, n):
        return w[name][rows[0]:rows[1], at:at + n].rearrange("(k p) n -> p k n", p=P)

    units = []

    def ffn(f):
        gate, up, down = f"ffn{f}_w_gate", f"ffn{f}_w_up", f"ffn{f}_w_down"
        for h in range(2):
            for j in range(HALF):
                at = (h * HALF + j) * P
                units.append((f"gu{f}", h * HALF + j, 2 * DC * P,
                              [(0, DC, P, cols(gate, (0, D), at, P)), (DC * P, DC, P, cols(up, (0, D), at, P))]))
            for c in range(DC):
                rows = (h * HALF * P, (h + 1) * HALF * P)
                units.append((f"down{f}", h * DC + c, HALF * P, [(0, HALF, P, cols(down, rows, c * P, P))]))

    def w_in(kind, i, at, n):
        units.append((kind, i, DC * n, [(0, DC, n, cols("w_in", (0, D), at, n))]))

    ffn(1)
    for i, (at, n) in enumerate(TOKEN_COLS):
        w_in("tok", i, at, n)
    for g in range(2):
        w_in("tok", len(TOKEN_COLS) + g, OHI + 256 * g, 256)
        w_in("feat", 3 * g, OHF + 256 * g, 256)
        w_in("feat", 3 * g + 1, OHQ + 256 * g, 256)
        w_in("feat", 3 * g + 2, OHG + 256 * g, 256)
    for g in range(DC // 2):
        w_in("ga", g, OGA + 256 * g, 256)
        w_in("gb", g, OGB + 256 * g, 256)
        units.append(("proj", g, 8 * 256,
                      [(0, 4, 256, cols("w_proj_attn", (0, 512), 256 * g, 256)),
                       (4 * 256, 4, 256, cols("w_proj_hgrn", (0, 512), 256 * g, 256))]))
    for g in range(DC // 2):
        units.append(("out", g, DC * 256, [(0, DC, 256, cols("w_out", (0, D), 256 * g, 256))]))
    ffn(2)
    return units


TOKEN_COLS = [(OIQ, 256), (OIK, DI + HI), (OK_, 256), (OK_ + 256, 256), (OQ, 256), (OQ + 256, 256),
              (OV, 256), (OV + 256, 256)]


NTOK = len(TOKEN_COLS)
BIG = 1.0e30
OUT_OF_REACH = -3.3e38
TAKEN = -3.0e38


C_ID, C_ONE = 0, P
C_COS = C_ONE + P
C_SIN = C_COS + NT * HR
C_OWN = C_SIN + NT * HR
C_OTHER = C_OWN + NS
C_ROWS = C_OTHER + NS
C_NEW = C_ROWS + 4 * P
C_TRI = C_NEW + NQ
C_END = C_TRI + P
LEVELS = [0, 1, 2, 4, 8, 16, 32, 64]


def constants():
    c = np.zeros((P, C_END), np.float32)
    c[:, C_ID:C_ID + P] = np.eye(P)
    c[:, C_ONE:C_ONE + P] = 1
    inv = np.float32(THETA) ** (-np.arange(0, ROT, 2, dtype=np.float32) / np.float32(ROT))
    pos = np.zeros((P, NT), np.float32)
    pos[:NS, 0] = PAST + np.arange(NS) % NQ
    for t in range(1, NT):
        pos[:, t] = np.arange(P) + P * (t - 1)
    angle = pos[:, :, None] * inv.astype(np.float32)
    c[:, C_COS:C_SIN] = np.cos(angle.astype(np.float32)).reshape(P, -1)
    c[:, C_SIN:C_OWN] = np.sin(angle.astype(np.float32)).reshape(P, -1)
    own = np.kron(np.eye(NB), np.ones((NQ, NQ)))
    c[:NS, C_OWN:C_OWN + NS] = own
    c[:NS, C_OTHER:C_OTHER + NS] = (own - 1) * BIG
    for pair in range(4):
        for r in range(P):
            c[(2 * pair + r // 16 % 2) * NQ + r % NQ, C_ROWS + pair * P + r] = 1
    q, j = np.arange(NS)[:, None] % NQ, np.arange(NQ)[None]
    c[:NS, C_NEW:C_NEW + NQ] = np.where(j <= q, 0, OUT_OF_REACH)
    q, j = np.arange(P)[:, None], np.arange(P)[None]
    c[:, C_TRI:C_TRI + P] = np.where(j <= q, 0, OUT_OF_REACH)
    return c


def level_masks():
    s, t = np.arange(P)[:, None], np.arange(P)[None]
    m = [s == t]
    for b in LEVELS[1:]:
        m.append((s // (2 * b) == t // (2 * b)) & (s // b % 2 == 0) & (t // b % 2 == 1))
    return np.stack(m, 1).astype(np.int32).reshape(P, -1)


def build(nc, w, out):
    units = weight_units(w)
    U = len(units)
    at_unit = {(kind, i): u for u, (kind, i, _, _) in enumerate(units)}

    def landed(u):
        return 16 * sum(len(units[v][3]) for v in range(u % NRAW, u + 1, NRAW))

    sems = {}
    with ExitStack() as ctx:
        def sem(name):
            if name not in sems:
                sems[name] = ctx.enter_context(nc.semaphore(name))
            return sems[name]

        place = [(nc.sbuf_base + 31) // 32 * 32]

        def sb(name, shape, dtype=F32, at=None):
            size = int(np.prod(shape[1:])) * (2 if dtype == BF16 else 4)
            size = (size + 31) // 32 * 32
            where = place[0] if at is None else at
            if at is None:
                place[0] += size
            assert where + size <= nc.sbuf_usable_end, (name, where + size)
            return nc.alloc_sbuf_tensor_at(name, shape, dtype, offset=where), where + size

        ps = ctx.enter_context(nc.psum_tensor("ps", [P, 8, 512], F32))
        flat = ps[:, :, :].rearrange("p b n -> p (b n)")

        cst, _ = sb("cst", [P, C_END])
        lmask, _ = sb("lmask", [P, len(LEVELS) * P], I32)
        gains, _ = sb("gains", [P, 3, DC])
        gain_q, _ = sb("gain_q", [P, 2, DH])
        bound, _ = sb("bound", [P, 2, HB])
        gain_o, _ = sb("gain_o", [P, 1])
        lbs, _ = sb("lbs", [P, 2, HB])
        pages, _ = sb("pages", [1, NB * NPG], I32)
        rows_b, _ = sb("rows_b", [NS, 4 * P], BF16)
        ident_b, _ = sb("ident_b", [P, P], BF16)
        n_hi, _ = sb("n_hi", [P, DC, T], F32R)
        n_lo, _ = sb("n_lo", [P, DC, T], F32R)
        raw, _ = sb("raw", [P, NRAW, UNIT])
        w_hi, _ = sb("w_hi", [P, NW, UNIT], F32R)
        w_lo, _ = sb("w_lo", [P, NW, UNIT], F32R)
        small, _ = sb("small", [P, 96])
        stat, _ = sb("stat", [P, 16])
        eps_col = small[:, 63:64]
        x_at = place[0]
        xT, _ = sb("xT", [P, DC, T])
        qT, e = sb("qT", [P, 4, T], at=x_at)
        kT, _ = sb("kT", [P, 4, T], at=e)
        free_at = place[0]
        hid_hi, e = sb("hid_hi", [P, HALF, T], F32R, at=free_at)
        hid_lo, e = sb("hid_lo", [P, HALF, T], F32R, at=e)
        sg, e = sb("sg", [P, 2, T], at=e)
        hf, e = sb("hf", [P, T], at=e)
        ffn_end = e
        sq, e = sb("sq", [P, 2, T], at=ffn_end)
        sqsum, e = sb("sqsum", [P, T], at=e)
        rms, e = sb("rms", [P, T], at=e)
        nf, e = sb("nf", [P, 2, T], at=e)
        xin, _ = sb("xin", [P, NT, D], at=free_at)
        stage, e = sb("stage", [P, 2, NT, 256], at=free_at)
        score_s, e = sb("score_s", [NS, PAST + NQ], at=e)
        score_p, bias_at = sb("score_p", [P, 256 + 384 + 512], at=e)
        bias_s, e = sb("bias_s", [NS, PAST + NS], BF16, at=bias_at)
        bias_p, e = sb("bias_p", [P, 128 + 256 + 384 + 512], BF16, at=e)
        iw_tok, e = sb("iw_tok", [P, NT, HI], at=e)
        oT, e = sb("oT", [P, HB, T], at=e)
        mix_at = e
        iqT, e = sb("iqT", [DI, HI, T], at=mix_at)
        ikT, e = sb("ikT", [DI, T], at=e)
        tmp, e = sb("tmp", [P, NT * 256], at=e)
        ipage, e = sb("ipage", [P, 3, NB * 4, DI], at=e)
        ipT, e = sb("ipT", [DI, 4, 512], at=e)
        rel, e = sb("rel", [P, 2, 512], at=mix_at - 4 * HB * T)
        pick, e = sb("pick", [NS, 2, P], at=e)
        weigh, e = sb("weigh", [P, 2, NS], at=e)
        newsc, e = sb("newsc", [NS, 2, NS], at=e)
        iq_s, e = sb("iq_s", [DI, NB, HI * NQ], at=e)
        decay, e = sb("decay", [P, 2, T], at=mix_at)
        key, e = sb("key", [P, 2, T], at=e)
        query, e = sb("query", [P, 2, T], at=e)
        out_gate, e = sb("out_gate", [P, 4, T], at=e)
        left, e = sb("left", [P, T], at=e)
        q_lev, e = sb("q_lev", [P, 2, T], at=e)
        k_lev, e = sb("k_lev", [P, 2, T], at=e)
        att, e = sb("att", [P, 4, P], at=e)
        att_s, e = sb("att_s", [NS, NS], at=e)
        k_rows, e = sb("k_rows", [P, NT, KD], at=e)
        state, e = sb("state", [P, 2, VD], at=e)
        state_s, e = sb("state_s", [P, NB, VD], at=e)
        v_own, e = sb("v_own", [NS, NB, VD], at=e)
        o_sq, e = sb("o_sq", [P, 2, T], at=free_at)
        o_rms, e = sb("o_rms", [P, T], at=e)
        aT, a_end = sb("aT", [P, 4, T], at=free_at)
        v_new, vn_end = sb("v_new", [NS, HA * DH], at=a_end)
        v_tok, e = sb("v_tok", [P, 4, HA * DH], at=mix_at)
        prob_p, e = sb("prob_p", [P, 2, SEQ], at=e)
        probT_p, e = sb("probT_p", [P, 2, 4, P], at=e)
        K_RING, V_RING = 3, 5
        KP_BANK = (4, 5, 7)
        k_page, e = sb("k_page", [P, K_RING, 4, HA * DH], at=mix_at)
        kpT, e = sb("kpT", [P, 3, 512], at=e)
        v_page, e = sb("v_page", [P, V_RING, HA * DH], at=e)
        prob, e = sb("prob", [P, PAST + NS], at=e)
        probT, e = sb("probT", [P, 2, 4, P], at=vn_end)
        probT_new, e = sb("probT_new", [NS, P], at=e)
        q_blk, e = sb("q_blk", [P, 4, 4, 2, 32], at=e)
        o_rows, e = sb("o_rows", [P, 2, P], at=e)
        assert e <= bias_at
        a_hi, e = sb("a_hi", [P, 4, T], F32R, at=free_at + 41 * 1024)
        a_lo, e = sb("a_lo", [P, 4, T], F32R, at=e)
        o_hi, e = sb("o_hi", [P, 4, T], F32R, at=e)
        o_lo, e = sb("o_lo", [P, 4, T], F32R, at=e)
        gate_a, e = sb("gate_a", [P, 2, T], at=e)
        gate_b, e = sb("gate_b", [P, 2, T], at=e)
        m_hi, e = sb("m_hi", [P, DC, T], F32R, at=free_at)
        m_lo, e = sb("m_lo", [P, DC, T], F32R, at=e)
        part_a, e = sb("part_a", [P, T], at=e)
        part_b, e = sb("part_b", [P, T], at=e)
        assert e <= free_at + 41 * 1024
        yout, _ = sb("yout", [P, NT, D], at=free_at)

        ident = cst[:, C_ID:C_ID + P]
        ones = cst[:, C_ONE:C_ONE + P]
        scratch_x = nc.dram_tensor("scratch_x", (P, DC * T), F32, kind="Internal").ap()

        def bank_pair(b):
            return ps[:, b:b + 2, 0:HT]

        def halves(ap):
            return ap.rearrange("p (h t) -> p h t", h=2)

        TURNS, TURNS_OF = [], [[] for _ in range(NTOK)]
        for i, (at, n) in enumerate(TOKEN_COLS):
            if at == OIQ:
                new = [(DI, iqT[:, h, :], slice(h * DI, (h + 1) * DI)) for h in range(HI)]
            elif at == OIK:
                new = [(DI, ikT[:, :], slice(0, DI))]
            elif at < OV:
                first = (at - (OK_ if at >= OK_ else OQ)) // P
                dst = kT if at >= OK_ else qT
                new = [(P, dst[:, first + a, :], slice(a * P, (a + 1) * P)) for a in range(2)]
            else:
                new = []
            TURNS_OF[i] = list(range(len(TURNS), len(TURNS) + len(new)))
            TURNS += new

        def stores(i):
            at, n = TOKEN_COLS[i]
            if at == OIK:
                pairs = [(out[4][0, 0].rearrange("(t p) d -> p t d", p=P), out[8][0].rearrange("b q d -> (b q) d"), DI)]
            elif OK_ <= at < OIQ:
                p, s = (out[2], out[6]) if at < OV else (out[3], out[7])
                part = slice((at - (OK_ if at < OV else OV)), (at - (OK_ if at < OV else OV)) + n)
                pairs = [(p[0, 0].rearrange("(t p) h d -> p t (h d)", p=P)[:, :, part],
                          s[0].rearrange("b q h d -> (b q) (h d)")[:, part], n)]
            else:
                pairs = []
            return [x for prompt, sample, m in pairs
                    for x in ((prompt, stage[:, i % 2, 1:NT, :m]), (sample, stage[0:NS, i % 2, 0, :m]))]

        STORED_BEFORE = [16 * sum(len(stores(v)) for v in range(i % 2, i, 2)) for i in range(NTOK + 2)]

        block = ctx.enter_context(nc.Block())
        S = sem

        def linker(eng, name):
            chain = S(name)
            count = [0]

            def link(ins):
                count[0] += 1
                ins.then_inc(chain, 1)
                eng.wait_ge(chain, count[0])
            return link

        def rows(t):
            return NS if t == 0 else P

        def cols(t):
            return slice(TILE_AT[t], TILE_AT[t] + rows(t))

        X_READ, X_FFN1, X_OUT, X_FFN2 = DC, 3 * DC, 4 * DC, 6 * DC
        DOWN_BANK = [4, 6, 0, 2, 0, 2, 4, 6]
        NORM_BASE = [0, X_FFN1 - DC, X_OUT - DC]

        N_POOL = w["cache_idx_k"].shape[0]
        SMALL_IN = 16 * 7
        SCORE_AT = {2: 0, 3: 256, 4: 640}
        GROUPS = 4 * NB

        @block.sync
        def _(sp):
            sp.dma_start(cst[:, :], w["cst"]).then_inc(S("cst_in"), 16)
            sp.dma_start(xin[0:NS, 0, :], w["x_sample"].rearrange("b q d -> (b q) d")).then_inc(S("x_in"), 16)
            sp.dma_start(xin[:, 1:NT, :], w["x_prompt"][0].rearrange("(t p) d -> p t d", p=P)).then_inc(S("x_in"), 16)
            sp.dma_start(gains[:, :, :], w["gains"]).then_inc(S("small_in"), 16)
            for n, name in enumerate(("q_norm", "k_norm")):
                sp.dma_start(gain_q[:, n, :], w[name].partition_broadcast(P)).then_inc(S("small_in"), 16)
            sp.dma_start(lbs[:, :, :], w["lbs"]).then_inc(S("small_in"), 16)
            sp.dma_start(gain_o[:, :], w["gain_o"]).then_inc(S("small_in"), 16)
            sp.dma_start(pages[:, :], w["page_table"].rearrange("b n -> (b n)").rearrange("(a n) -> a n", a=1)).then_inc(S("small_in"), 16)
            sp.dma_start(lmask[:, :], w["lmask"]).then_inc(S("small_in"), 16)

            def index_pages(kc):
                if kc == 3:
                    sp.wait_ge(S("ip_turned"), NB)
                if kc == 0:
                    sp.wait_ge(S("n_done"), 2 * DC)
                for b in range(NB):
                    for n in range(4):
                        page = sp.value_load(pages[0:1, b * NPG + 4 * kc + n:b * NPG + 4 * kc + n + 1],
                                             min_val=0, max_val=N_POOL - 1)
                        sp.dma_start(ipage[:, kc % 3, 4 * b + n, :],
                                     w["cache_idx_k"][bass.ds(page, 1), :, :].rearrange("a p d -> (a p) d")
                                     ).then_inc(S(f"ip_in{kc % 2}"), 16)

            def load_page(dst, cache, b, n):
                page = sp.value_load(pages[0:1, b * NPG + n:b * NPG + n + 1], min_val=0, max_val=N_POOL - 1)
                return sp.dma_start(dst, w[cache][bass.ds(page, 1)].rearrange("a p h d -> (a p) (h d)"))

            def attention_pages(pair):
                if pair == 0:
                    sp.wait_ge(S("pa_out"), 16)
                    sp.wait_ge(S("state_s_out"), 16 * HB)
                for n in range(8):
                    m = 8 * pair + n
                    if m >= K_RING:
                        sp.wait_ge(S("kp_turned"), 4 * (m - K_RING + 1))
                    for j in range(4):
                        load_page(k_page[:, m % K_RING, j, :], "cache_k", 2 * pair + n % 2,
                                  4 * (n // 2) + j).then_inc(S(f"k_in{m % K_RING}"), 16)
                for n in range(2 * NPG):
                    m = 2 * NPG * pair + n
                    if m >= V_RING:
                        sp.wait_ge(S("v_used"), m - V_RING + 1)
                    load_page(v_page[:, m % V_RING, :], "cache_v", 2 * pair + n % 2,
                              n // 2).then_inc(S(f"v_in{m % V_RING}"), 16)

            for u in range(U):
                if u == at_unit["proj", 0]:
                    for pair in range(4):
                        attention_pages(pair)
                if u == at_unit["tok", 3]:
                    sp.wait_ge(S("small_in"), SMALL_IN)
                    index_pages(0)
                    index_pages(1)
                if u == at_unit["tok", 5]:
                    index_pages(2)
                    index_pages(3)
                if u >= NRAW:
                    sp.wait_ge(S("w_lo_done"), u - NRAW + 1)
                for at, k, n, src in units[u][3]:
                    dst = raw[:, u % NRAW, at:at + k * n].rearrange("p (k n) -> p k n", k=k)
                    sp.dma_start(dst, src).then_inc(S(f"w_landed{u % NRAW}"), 16)


        @block.gpsimd
        def _(pool):
            pool.memset(eps_col, EPS).then_inc(S("eps_in"), 1)
            done = [0]

            def lows(last):
                while done[0] <= min(last, U - 1):
                    u = done[0]
                    n = units[u][2]
                    pool.wait_ge(S("w_hi_done"), u + 1)
                    pool.tensor_tensor(w_lo[:, u % NW, :n], raw[:, u % NRAW, :n], w_hi[:, u % NW, :n].bitcast(F32),
                                       ALU.subtract).then_inc(S("w_lo_done"), 1)
                    done[0] += 1

            def head_state(h):
                if h == 0:
                    pool.wait_ge(S("index_done"), 1)
                pool.dma_start(state_s[:, :, :], w["state_hgrn"][:, h].rearrange("b k v -> k b v")).then_inc(S("state_in"), 16)
                pool.wait_ge(S("state_s_done"), h + 1)
                pool.dma_start(out[9][0, :, h].rearrange("b k v -> k b v"), state_s[:, :, :]).then_inc(S("state_s_out"), 16)
                pool.wait_ge(S("state_s_out"), 16 * (h + 1))

            for g in range(2):
                lows(at_unit["feat", 3 * g + 2] + 2)
                head_state(2 * g)
                head_state(2 * g + 1)
            lows(U)

        @block.scalar
        def _(act):
            done = [0]

            def split(last):
                while done[0] <= min(last, U - 1):
                    u = done[0]
                    n = units[u][2]
                    act.wait_ge(S(f"w_landed{u % NRAW}"), landed(u))
                    if u >= NW:
                        act.wait_ge(S("unit_done"), u - NW + 1)
                    act.activation(w_hi[:, u % NW, :n], raw[:, u % NRAW, :n], ACT.Copy).then_inc(S("w_hi_done"), 1)
                    done[0] += 1

            def square(k, c):
                act.wait_ge(S("x_version"), NORM_BASE[k] + c + 1)
                if DC * k + c >= 2:
                    act.wait_ge(S("sq_added"), DC * k + c - 1)
                act.activation(sq[:, c % 2, :], xT[:, c, :], ACT.Square).then_inc(S("sq_done"), 1)

            def norm(k):
                act.wait_ge(S("ss_done"), k + 1)
                act.activation(halves(rms[:, :]), bank_pair(0), ACT.Sqrt, scale=1.0 / D,
                               bias=eps_col).then_inc(S("rms_done"), 1)
                for c in range(DC):
                    act.wait_ge(S("nf_done"), DC * k + c + 1)
                    act.activation(n_hi[:, c, :], nf[:, c % 2, :], ACT.Copy).then_inc(S("n_hi_done"), 1)

            def ffn(f, G0, k_next):
                for h in range(2):
                    for j in range(HALF):
                        u = at_unit[f"gu{f}", h * HALF + j]
                        G = G0 + h * HALF + j
                        split(u + 1)
                        act.wait_ge(S("unit_done"), u + 1)
                        if G >= 2:
                            act.wait_ge(S("hid_done"), G - 1)
                        act.activation(halves(sg[:, G % 2, :]), bank_pair(4 * (j % 2)),
                                       ACT.Silu).then_inc(S("gate_done"), 1)
                    for c in range(DC):
                        split(at_unit[f"down{f}", h * DC + c] + 1)
                        if h == 1 and c and k_next is not None:
                            square(k_next, c - 1)
                if k_next is not None:
                    square(k_next, DC - 1)

            def token_major():
                for i in range(NTOK):
                    u = at_unit["tok", i]
                    n = TOKEN_COLS[i][1]
                    split(u + 1)
                    act.wait_ge(S("unit_done"), u + 1)
                    if STORED_BEFORE[i]:
                        act.wait_ge(S(f"stored{i % 2}"), STORED_BEFORE[i])
                    act.activation(stage[:, i % 2, :, :n],
                                   flat[:, 1536 * (i % 2):1536 * (i % 2) + NT * 256]
                                   .rearrange("p (t n) -> p t n", t=NT)[:, :, :n],
                                   ACT.Copy).then_inc(S("stage_done"), 1)
                    if i == 3:
                        turn_out(2)
                        index()
                    if OK_ == TOKEN_COLS[i][0] // 512 * 512 or OQ == TOKEN_COLS[i][0] // 512 * 512:
                        act.wait_ge(S("qk_ss"), i - 1)
                        act.activation(small[:, 20:40], small[:, 0:20], ACT.Sqrt, scale=1.0 / DH,
                                       bias=eps_col).then_inc(S("qk_rms"), 1)
                    if i != 3:
                        turn_out(i - 1)

            def turn_out(i):
                if i >= 0:
                    act.wait_ge(S("tok_done"), i + 1)
                    for dst, src in stores(i):
                        act.dma_start(dst, src).then_inc(S(f"stored{i % 2}"), 16)
                if i == 2:
                    act.wait_ge(S("x_spilled"), 16)
                for m in TURNS_OF[i] if i >= 0 else []:
                    n, dst, _ = TURNS[m]
                    act.wait_ge(S("turned"), m + 1)
                    act.activation(dst[:, NS:T], ps[0:n, 6, 0:SEQ], ACT.Copy)
                    act.activation(dst[:, 0:NS], ps[0:n, 7, 0:NS], ACT.Copy).then_inc(S("turned_out"), 1)

            def index():
                for n in range(GROUPS):
                    if n % 2 == 0:
                        act.wait_ge(S("ip_turned"), n + 1)
                        if n >= 4:
                            act.wait_ge(S("dots_done"), n - 3)
                        act.activation(ipT[:, n % 4, :], ps[0:DI, n % 2, :], ACT.Copy).then_inc(S("ip_even"), 1)
                    if n % 4 == 3:
                        act.wait_ge(S("dots_done"), n + 1)
                        if n >= 8:
                            act.wait_ge(S("weighed"), n // 4 - 1)
                        act.activation(rel[:, n // 4 % 2, :], ps[:, 4 + n // 4 % 2, :], ACT.Relu).then_inc(S("rel_done"), 1)
                act.wait_ge(S("new_dots"), 1)
                act.activation(rel[:, 0, 0:2 * NS], ps[:, 7, 0:2 * NS], ACT.Relu).then_inc(S("rel_new"), 1)
                for m in range(12):
                    width = P * (2 + m // 4)
                    act.wait_ge(S("p_dots"), m + 1)
                    if m >= 2:
                        act.wait_ge(S("p_scored"), m - 1)
                    act.activation(rel[:, m % 2, :width], ps[:, 4 + m % 2, :width], ACT.Relu).then_inc(S("p_rel"), 1)

            def features(g):
                i = NTOK + g
                split(at_unit["tok", i] + 1)
                act.wait_ge(S("unit_done"), at_unit["tok", i] + 1)
                if g == 0:
                    act.wait_ge(S("stored0"), STORED_BEFORE[i])
                else:
                    act.wait_ge(S("stored1"), STORED_BEFORE[i])
                act.activation(stage[:, i % 2, :, :], flat[:, 2560:2560 + NT * 256]
                               .rearrange("p (t n) -> p t n", t=NT), ACT.Copy).then_inc(S("stage_done"), 1)
                for r in range(3):
                    u = at_unit["feat", 3 * g + r]
                    split(u + 1)
                    act.wait_ge(S("unit_done"), u + 1)
                    if r == 0:
                        act.wait_ge(S("head_read"), 2 * g) if g else act.wait_ge(S("index_done"), 1)
                        if g:
                            act.wait_ge(S("state_s_done"), 2)
                    for a in range(2):
                        src = bank_pair(4 * (r % 2) + 2 * a)
                        if r == 0:
                            act.activation(halves(decay[:, a, :]), src, ACT.Sigmoid)
                            ins = act.activation(halves(key[:, a, :]), src, ACT.Sigmoid, scale=-1.0)
                        elif r == 1:
                            ins = act.activation(halves(query[:, a, :]), src, ACT.Silu)
                        else:
                            ins = act.activation(halves(out_gate[:, 2 * g + a, :]), src, ACT.Silu)
                        ins.then_inc(S("feat_done"), 1)
                split(at_unit["feat", 3 * g + 2] + 2)

            def head(h):
                act.wait_ge(S("k_turned"), h + 1)
                act.activation(k_rows[:, 1:NT, :], ps[:, 4, :].rearrange("p (t k) -> p t k", t=4), ACT.Copy)
                act.activation(k_rows[0:NS, 0, :], ps[0:NS, 6, 0:KD], ACT.Copy).then_inc(S("k_rows_done"), 1)
                act.wait_ge(S("o_summed"), h + 1)
                act.activation(oT[:, h, NS:T], ps[:, 0, :], ACT.Copy)
                act.activation(oT[:, h, 0:NS], ps[:, 1, 0:NS], ACT.Copy).then_inc(S("o_out"), 1)
                act.wait_ge(S("state_done"), 4 * h + 4)
                act.dma_start(out[5][0, 0, h], state[:, 1, :]).then_inc(S("state_out"), 16)

            def output_norm():
                act.wait_ge(S("o_out"), HB)
                act.wait_ge(S("head_read"), HB)
                for h in range(HB):
                    if h >= 2:
                        act.wait_ge(S("o_sq_used"), h - 1)
                    act.activation(o_sq[:, h % 2, :], oT[:, h, :], ACT.Square).then_inc(S("o_sq_done"), 1)
                act.wait_ge(S("o_sq_used"), HB)
                act.activation(halves(o_rms[:, :]), bank_pair(0), ACT.Sqrt, scale=1.0 / VD,
                               bias=eps_col).then_inc(S("o_rms_done"), 1)

            def prompt_attention():
                act.wait_ge(S("o_scaled"), HB)
                act.wait_ge(S("state_s_out"), 16 * HB)
                act.dma_start(v_tok[:, :, :], out[3][0, 0].rearrange("(t p) h d -> p t (h d)", p=P)).then_inc(S("v_back"), 16)

                def turned(n):
                    t = 1 + n // HA
                    act.wait_ge(S("pp_turned"), n + 1)
                    if n >= 2:
                        act.wait_ge(S("pv_done"), n - 1)
                    act.activation(probT_p[:, n % 2, 0:t, :], ps[:, 2 + n % 2, 0:P * t]
                                   .rearrange("p (s q) -> p s q", s=t), ACT.Copy).then_inc(S("ppT_done"), 1)

                for n in range(4 * HA):
                    width = P * (1 + n // HA)
                    act.wait_ge(S("pp_max"), n + 1)
                    if n >= 2:
                        act.wait_ge(S("pp_turned"), n - 1)
                    act.activation(prob_p[:, n % 2, :width], ps[:, n % 2, :width], ACT.Exp, scale=DH ** -0.5,
                                   bias=stat[:, 4 * (n % 2) + 1:4 * (n % 2) + 2],
                                   accum_out=stat[:, 4 * (n % 2) + 2:4 * (n % 2) + 3]).then_inc(S("pp_exp"), 1)
                    if n:
                        turned(n - 1)
                turned(4 * HA - 1)

            def sample_attention():
                act.wait_ge(S("biased"), 1)
                act.dma_start(v_new[:, :], out[7][0].rearrange("b q h d -> (b q) (h d)")).then_inc(S("v_new_back"), 16)
                for pair in range(4):
                    for n in range(0, 32, 2):
                        m = 32 * pair + n
                        act.wait_ge(S("kp_turned"), m + 1)
                        if m >= 3:
                            act.wait_ge(S("kp_used"), m - 2)
                        act.activation(kpT[:, m % 3, :], ps[:, KP_BANK[m % 3], :], ACT.Copy).then_inc(S("kpT_even"), 1)
                    act.wait_ge(S("sp_max"), pair + 1)
                    if pair:
                        act.wait_ge(S("spn_turned"), pair)
                        act.wait_ge(S("sp_turned"), 4 * pair)
                    act.activation(prob[:, 0:PAST], flat[:, 0:PAST], ACT.Exp, scale=DH ** -0.5, bias=stat[:, 9:10],
                                   accum_out=stat[:, 10:11])
                    act.activation(prob[:, PAST:], ps[:, 6, 0:NS], ACT.Exp, scale=DH ** -0.5, bias=stat[:, 9:10],
                                   accum_out=stat[:, 11:12]).then_inc(S("sp_exp"), 1)
                    for j in range(4):
                        m = 4 * pair + j
                        act.wait_ge(S("sp_turned"), m + 1)
                        if m >= 2:
                            act.wait_ge(S("v_used"), 8 * (m - 1))
                        act.activation(probT[:, m % 2, :, :], ps[:, 4 + j % 2, :].rearrange("p (s r) -> p s r", s=4),
                                       ACT.Copy).then_inc(S("spT_done"), 1)

            def projections():
                for g in range(DC // 2):
                    for name, gate, bank in (("ga", gate_a, 0), ("gb", gate_b, 4)):
                        u = at_unit[name, g]
                        split(u + 1)
                        act.wait_ge(S("unit_done"), u + 1)
                        if g:
                            act.wait_ge(S("merged"), 2 * g)
                        else:
                            act.wait_ge(S("aT_done"), 4)
                        for a in range(2):
                            ins = act.activation(halves(gate[:, a, :]), bank_pair(bank + 2 * a), ACT.Sigmoid)
                        ins.then_inc(S(name + "_done"), 1)
                    split(at_unit["proj", g] + 1)
                for g in range(DC // 2):
                    split(at_unit["out", g] + 1)
                    if g:
                        square(2, 2 * g - 2)
                        square(2, 2 * g - 1)
                square(2, DC - 2)
                square(2, DC - 1)

            act.wait_ge(S("eps_in"), 1)
            split(0)
            for c in range(DC):
                square(0, c)
            norm(0)
            act.wait_ge(S("bound_in"), 1)
            act.activation(bound[:, :, :], bound[:, :, :], ACT.Sigmoid).then_inc(S("bound_done"), 1)
            ffn(1, 0, 1)
            act.wait_ge(S("x_version"), X_FFN1)
            act.dma_start(scratch_x, xT[:, :, :].rearrange("p c t -> p (c t)")).then_inc(S("x_spilled"), 16)
            norm(1)
            token_major()
            turn_out(NTOK - 1)
            for m in range(2):
                act.wait_ge(S(f"stored{m}"), 16 * sum(len(stores(v)) for v in range(m, NTOK, 2)))
            for g in range(2):
                features(g)
                head(2 * g)
                head(2 * g + 1)
            act.wait_ge(S("state_out"), 16 * HB)
            output_norm()
            prompt_attention()
            sample_attention()
            act.wait_ge(S("aT_done"), 4)
            act.dma_start(xT[:, :, :].rearrange("p c t -> p (c t)"), scratch_x).then_inc(S("x_back"), 16)
            projections()
            norm(2)
            ffn(2, 2 * HALF, None)
            for c in range(DC):
                act.wait_ge(S("y_turned"), c + 1)
                act.activation(yout[0:NS, 0, c * P:(c + 1) * P], ps[0:NS, 2 * (c % 4) + 1, 0:P],
                               ACT.Copy).then_inc(S("y_out_s"), 1)
            act.wait_ge(S("y_out_s"), DC)
            act.dma_start(out[1].rearrange("b q d -> (b q) d"), yout[0:NS, 0, :]).then_inc(S("y_stored"), 16)
            act.wait_ge(S("y_out_p"), DC)
            act.dma_start(out[0][0].rearrange("(t p) d -> p t d", p=P), yout[:, 1:NT, :]).then_inc(S("y_stored"), 16)
            act.wait_ge(S("y_stored"), 32)

        @block.vector
        def _(dve):
            link = linker(dve, "dve_chain")

            def x_in():
                for c in range(DC):
                    dve.wait_ge(S("x_turned"), c + 1)
                    dve.tensor_copy(xT[:, c, NS:T], ps[:, 2 * (c % 4), 0:SEQ])
                    dve.tensor_copy(xT[:, c, 0:NS], ps[:, 2 * (c % 4) + 1, 0:NS]).then_inc(S("x_version"), 1)
                    sq_add(0, c)

            def sq_add(k, c):
                n = DC * k + c
                dve.wait_ge(S("sq_done"), n + 1)
                if c == 0:
                    dve.tensor_copy(sqsum[:, :], sq[:, 0, :]).then_inc(S("sq_added"), 1)
                else:
                    dve.wait_ge(S("sq_added"), n)
                    dve.tensor_tensor(sqsum[:, :], sqsum[:, :], sq[:, c % 2, :], ALU.add).then_inc(S("sq_added"), 1)

            def norm(k):
                dve.wait_ge(S("rms_done"), k + 1)
                if k == 0:
                    dve.wait_ge(S("small_in"), SMALL_IN)
                link(dve.reciprocal(rms[:, :], rms[:, :]))
                for c in range(DC):
                    n = DC * k + c
                    if c >= 2:
                        dve.wait_ge(S("n_done"), n - 1)
                    dve.scalar_tensor_tensor(nf[:, c % 2, :], xT[:, c, :], gains[:, k, c:c + 1], rms[:, :],
                                             ALU.mult, ALU.mult).then_inc(S("nf_done"), 1)
                    dve.wait_ge(S("n_hi_done"), n + 1)
                    dve.tensor_tensor(n_lo[:, c, :], nf[:, c % 2, :], n_hi[:, c, :].bitcast(F32),
                                      ALU.subtract).then_inc(S("n_done"), 1)

            def ffn(f, G0, x0, k_next):
                for h in range(2):
                    for j in range(HALF):
                        u = at_unit[f"gu{f}", h * HALF + j]
                        G = G0 + h * HALF + j
                        dve.wait_ge(S("unit_done"), u + 1)
                        dve.wait_ge(S("gate_done"), G + 1)
                        if G:
                            dve.wait_ge(S("hid_done"), G)
                        link(dve.tensor_tensor(halves(hf[:, :]), halves(sg[:, G % 2, :]),
                                               bank_pair(4 * (j % 2) + 2), ALU.mult))
                        link(dve.tensor_copy(hid_hi[:, j, :], hf[:, :]))
                        dve.tensor_tensor(hid_lo[:, j, :], hf[:, :], hid_hi[:, j, :].bitcast(F32),
                                          ALU.subtract).then_inc(S("hid_done"), 1)
                    for c in range(DC):
                        dve.wait_ge(S("unit_done"), at_unit[f"down{f}", h * DC + c] + 1)
                        if h == 1:
                            dve.wait_ge(S("x_version"), x0 + c + 1)
                        dve.scalar_tensor_tensor(halves(xT[:, c, :]), bank_pair(DOWN_BANK[c]), 0.5,
                                                 halves(xT[:, c, :]), ALU.mult, ALU.add).then_inc(S("x_version"), 1)
                        if h == 1 and k_next is not None:
                            sq_add(k_next, c)

            def rope(x, heads):
                cos = cst[:, C_COS:C_SIN].rearrange("p (t r) -> p t r", t=NT).unsqueeze(2).to_broadcast([P, NT, heads, HR])
                sin = cst[:, C_SIN:C_OWN].rearrange("p (t r) -> p t r", t=NT).unsqueeze(2).to_broadcast([P, NT, heads, HR])
                a, b, c, d = (tmp[:, m * 160:m * 160 + NT * heads * HR].rearrange("p (t h r) -> p t h r", t=NT, h=heads)
                              for m in range(4))
                x1, x2 = x[:, :, :, 0:HR], x[:, :, :, HR:ROT]
                dve.tensor_tensor(a, x1, cos, ALU.mult)
                dve.tensor_tensor(b, x2, sin, ALU.mult)
                dve.tensor_tensor(c, x2, cos, ALU.mult)
                link(dve.tensor_tensor(d, x1, sin, ALU.mult))
                dve.tensor_tensor(x1, a, b, ALU.subtract)
                return dve.tensor_tensor(x2, c, d, ALU.add)

            def token_major():
                for i, (at, n) in enumerate(TOKEN_COLS):
                    if i == 3:
                        index()
                    if i > 3:
                        take(4 if at < OV else 14)
                    dve.wait_ge(S("stage_done"), i + 1)
                    if i:
                        dve.wait_ge(S("tok_done"), i)
                    x = stage[:, i % 2, :, :]
                    if at == OIQ:
                        rope(x.rearrange("p t (h d) -> p t h d", h=HI), HI).then_inc(S("tok_done"), 1)
                    elif at == OIK:
                        link(rope(x[:, :, 0:DI].unsqueeze(2), 1))
                        dve.tensor_scalar(iw_tok[:, :, :], x[:, :, DI:DI + HI], IDX_SCALE, None,
                                          ALU.mult).then_inc(S("tok_done"), 1)
                    elif at < OV:
                        heads = x.rearrange("p t (h d) -> p (t h) d", d=DH)
                        t3 = tmp[:, :].rearrange("p (g d) -> p g d", d=DH)
                        g = gain_q[:, 1 if at >= OK_ else 0, :].unsqueeze(1).to_broadcast([P, NT * 4, DH])
                        link(dve.tensor_tensor(t3, heads, heads, ALU.mult))
                        dve.tensor_reduce(small[:, 0:20], t3, AX_X, ALU.add).then_inc(S("qk_ss"), 1)
                        dve.wait_ge(S("qk_rms"), i - 1)
                        link(dve.reciprocal(small[:, 40:60], small[:, 20:40]))
                        link(dve.tensor_tensor(heads, heads, small[:, 40:60].unsqueeze(2).to_broadcast([P, NT * 4, DH]),
                                               ALU.mult))
                        link(dve.tensor_tensor(heads, heads, g, ALU.mult))
                        rope(x.rearrange("p t (h d) -> p t h d", d=DH), 4).then_inc(S("tok_done"), 1)
                        dve.wait_ge(S("tok_done"), i + 1)
                    else:
                        dve.engine_nop().then_inc(S("tok_done"), 1)
                take(10)

            def index():
                for g in range(2):
                    spread = pick[:, g, :].rearrange("p (b h q) -> p b h q", b=4, h=HI)
                    mine = cst[0:NS, C_ID + 32 * g:C_ID + 32 * g + 32].rearrange("p (b q) -> p b q", b=4)
                    for h in range(HI):
                        ins = dve.tensor_scalar(spread[:, :, h, :], mine, iw_tok[0:NS, 0, h:h + 1], None, ALU.mult)
                dve.wait_ge(S("turned_out"), len(TURNS_OF[0]))
                dve.tensor_copy(iq_s[:, :, :].rearrange("p b (h q) -> p h b q", h=HI),
                                iqT[:, :, 0:NS].rearrange("p h (b q) -> p h b q", b=NB)).then_inc(S("picked"), 1)
                dve.wait_ge(S("pick_turned"), 1)
                dve.tensor_copy(weigh[:, :, :], ps[:, 6, 0:2 * NS].rearrange("p (g n) -> p g n", g=2)).then_inc(S("weigh_done"), 1)

                def score_out(kc):
                    dve.wait_ge(S("weighed"), 2 * kc + 2)
                    dve.tensor_copy(score_s[:, 512 * kc:512 * kc + 512], ps[0:NS, 2 + kc % 2, :]).then_inc(S("scored"), 1)

                for n in range(GROUPS):
                    if n % 2 == 1:
                        dve.wait_ge(S("ip_turned"), n + 1)
                        if n >= 4:
                            dve.wait_ge(S("dots_done"), n - 3)
                        dve.tensor_copy(ipT[:, n % 4, :], ps[0:DI, n % 2, :]).then_inc(S("ip_odd"), 1)
                    if n % NB == 5 and n >= NB:
                        score_out(n // NB - 1)
                score_out(3)
                dve.wait_ge(S("new_weighed"), 1)
                link(dve.tensor_tensor(newsc[:, 0, :], cst[0:NS, C_OWN:C_OWN + NS], ps[0:NS, 6, 128:128 + NS], ALU.mult))
                link(dve.tensor_reduce(newsc[:, 1, 0:NQ], newsc[:, 0, :].rearrange("p (b j) -> p j b", b=NB), AX_X, ALU.add))
                link(dve.tensor_tensor(score_s[:, PAST:PAST + NQ], newsc[:, 1, 0:NQ], cst[0:NS, C_NEW:C_NEW + NQ], ALU.add))
                for m in range(12):
                    t, h = 2 + m // 4, m % 4
                    width = P * t
                    dst = score_p[:, SCORE_AT[t]:SCORE_AT[t] + width]
                    dve.wait_ge(S("p_rel"), m + 1)
                    if m:
                        dve.wait_ge(S("p_scored"), m)
                    if h == 0:
                        ins = dve.tensor_scalar(dst, rel[:, m % 2, :width], iw_tok[:, t, 0:1], None, ALU.mult)
                    else:
                        ins = dve.scalar_tensor_tensor(dst, rel[:, m % 2, :width], iw_tok[:, t, h:h + 1], dst,
                                                       ALU.mult, ALU.add)
                    ins.then_inc(S("p_scored"), 1)
                dve.wait_ge(S("p_scored"), 12)
                for t in range(2, NT):
                    dst = score_p[:, SCORE_AT[t] + P * (t - 1):SCORE_AT[t] + P * t]
                    ins = dve.tensor_tensor(dst, dst, cst[:, C_TRI:C_TRI + P], ALU.add)
                ins.then_inc(S("index_done"), 1)
                dve.wait_ge(S("index_done"), 1)

            searches = [(score_p[:, SCORE_AT[t]:SCORE_AT[t] + P * t], TOPK_P, P) for t in range(2, NT)]
            searches.append((score_s[:, :], TOPK_S, NS))
            PROMPT_ROUNDS = 3 * TOPK_P // 8
            ROUNDS = PROMPT_ROUNDS + TOPK_S // 8
            taken = [0]

            def take_half():
                n, second = divmod(taken[0], 2)
                for scores, k, r in searches:
                    if n < k // 8:
                        eight = small[0:r, 64:72]
                        if second:
                            link(dve.match_replace(scores, eight, scores, TAKEN))
                        else:
                            link(dve.max(eight, scores))
                        taken[0] += 1
                        return
                    n -= k // 8

            def take(rounds):
                for _ in range(2 * rounds):
                    take_half()

            def biases():
                take(PROMPT_ROUNDS - (taken[0] + 1) // 2)
                dve.tensor_scalar(bias_p[:, 0:P], cst[:, C_TRI:C_TRI + P], 0.0, -BIG, ALU.not_equal, ALU.mult)
                dve.tensor_scalar(bias_p[:, P:], score_p[:, :], TAKEN, -BIG, ALU.not_equal,
                                  ALU.mult).then_inc(S("prompt_biased"), 1)

            def sample_biases():
                take(ROUNDS)
                new = small[0:NS, 72:80]
                dve.tensor_scalar(bias_s[:, 0:PAST], score_s[:, 0:PAST], TAKEN, -BIG, ALU.not_equal, ALU.mult)
                link(dve.tensor_scalar(new, score_s[:, PAST:], TAKEN, -BIG, ALU.not_equal, ALU.mult))
                dve.tensor_tensor(bias_s[:, PAST:].rearrange("p (b j) -> p b j", b=NB),
                                  new.unsqueeze(1).to_broadcast([NS, NB, NQ]),
                                  cst[0:NS, C_OTHER:C_OTHER + NS].rearrange("p (b j) -> p b j", b=NB),
                                  ALU.add).then_inc(S("biased"), 1)

            def features(g):
                for a in range(2):
                    h = 2 * g + a
                    dve.wait_ge(S("feat_done"), 6 * g + a + 1)
                    dve.tensor_scalar(decay[:, a, :], decay[:, a, :], bound[:, 1, h:h + 1], bound[:, 0, h:h + 1],
                                      ALU.mult, ALU.add)
                    ins = dve.tensor_scalar(key[:, a, :], key[:, a, :], bound[:, 1, h:h + 1], None, ALU.mult)
                link(ins)
                take(4)
                dve.wait_ge(S("feat_done"), 6 * g + 4)
                if g == 0:
                    dve.memset(att[:, :, :], 0.0)
                    dve.memset(att_s[:, :], 0.0)
                    dve.memset(q_lev[:, :, :], 0.0)
                    link(dve.memset(k_lev[:, :, :], 0.0))
                dve.engine_nop().then_inc(S("feat_ready"), 1)

            def head(h):
                a, g = h % 2, h // 2
                dec, k, q = decay[:, a, :], key[:, a, :], query[:, a, :]

                def level_out(L):
                    dve.wait_ge(S("level_done"), 8 * h + L + 1)
                    m = lmask[:, L * P:(L + 1) * P]
                    if L:
                        dve.wait_ge(S("level_out"), 8 * h + L)
                    if LEVELS[L] < NQ:
                        dve.copy_predicated(att_s[:, :], lmask[0:NS, L * P:L * P + NS], ps[0:NS, 6 + L % 2, 0:NS])
                    dve.copy_predicated(att[:, :, :], m.unsqueeze(1).to_broadcast([P, 4, P]),
                                        ps[:, 4 + L % 2, :].rearrange("p (i t) -> p i t", i=4)).then_inc(S("level_out"), 1)

                if h:
                    dve.wait_ge(S("head_read"), h)
                for L in range(1, len(LEVELS)):
                    b = LEVELS[L]
                    at = 0 if 2 * b <= NQ else NS

                    def view(x):
                        return x[:, at:T].rearrange("p (n s b) -> p n s b", s=2, b=b)
                    if L >= 3:
                        dve.wait_ge(S("level_done"), 8 * h + L - 1)
                    right, first = view(dec)[:, :, 1, :], view(k)[:, :, 0, :]
                    n = right.shape[1]
                    dve.tensor_tensor(view(q_lev[:, L % 2, :])[:, :, 1, :], view(q)[:, :, 1, :], right, ALU.mult)
                    end = view(dec)[:, :, 1, b - 1:b].to_broadcast([P, n, b])
                    mid = view(dec)[:, :, 0, b - 1:b].to_broadcast([P, n, b])
                    into = view(k_lev[:, L % 2, :])[:, :, 0, :]
                    if L == 1:
                        dve.memset(left[:, :], 1.0)
                        dve.tensor_copy(into, first).then_inc(S("level_in"), 1)
                    else:
                        dve.tensor_tensor(into, first, view(left[:, :])[:, :, 0, :], ALU.mult).then_inc(S("level_in"), 1)
                    dve.wait_ge(S("level_in"), 8 * h + L)
                    link(dve.tensor_tensor(view(left[:, :])[:, :, 0, :], view(left[:, :])[:, :, 0, :], end, ALU.mult))
                    link(dve.tensor_tensor(right, right, mid, ALU.mult))
                    level_out(L - 1)
                dve.wait_ge(S("level_done"), 8 * h + 7)
                dve.tensor_tensor(q_lev[:, 0, :], q, dec, ALU.mult)
                dve.tensor_tensor(k_lev[:, 0, :], k, left[:, :], ALU.mult).then_inc(S("level_in"), 1)
                level_out(7)
                v0 = stage[0:NS, g, 0, a * VD:(a + 1) * VD]
                if h:
                    dve.wait_ge(S("head_read"), h)
                dve.tensor_tensor(v_own[:, :, :], v0.unsqueeze(1).to_broadcast([NS, NB, VD]),
                                  cst[0:NS, C_OWN:C_OWN + NS:NQ].unsqueeze(2).to_broadcast([NS, NB, VD]),
                                  ALU.mult).then_inc(S("v_own_done"), 1)
                for i in range(4):
                    dve.wait_ge(S("state_added"), 4 * h + i + 1)
                    if i == 1 and h:
                        dve.wait_ge(S("state_out"), 16 * h)
                    if i:
                        dve.wait_ge(S("state_done"), 4 * h + i)
                        if i >= 2:
                            dve.wait_ge(S("state_used"), 3 * h + i - 1)
                        dve.scalar_tensor_tensor(state[:, i % 2, :], state[:, (i + 1) % 2, :],
                                                 dec[:, NS + P * (i + 1) - 1:NS + P * (i + 1)], ps[:, 2 + i % 2, 0:VD],
                                                 ALU.mult, ALU.add).then_inc(S("state_done"), 1)
                    else:
                        dve.tensor_copy(state[:, 0, :], ps[:, 2, 0:VD]).then_inc(S("state_done"), 1)
                dve.wait_ge(S("o_summed"), h + 1)
                link(dve.tensor_tensor(state_s[:, :, :], state_s[:, :, :],
                                       dec[:, NQ - 1:NS:NQ].unsqueeze(2).to_broadcast([P, NB, VD]), ALU.mult))
                dve.wait_ge(S("head_read"), h + 1)
                for m in range(2):
                    part = state_s[:, 4 * m:4 * m + 4, :]
                    ins = dve.tensor_tensor(part, part, ps[:, 5 + 2 * m, :].rearrange("p (b v) -> p b v", b=4), ALU.add)
                ins.then_inc(S("state_s_done"), 1)

            def output_norm():
                dve.wait_ge(S("o_rms_done"), 1)
                dve.reciprocal(o_rms[:, :], o_rms[:, :]).then_inc(S("o_inv_done"), 1)
                for h in range(HB):
                    link(dve.scalar_tensor_tensor(oT[:, h, :], oT[:, h, :], gain_o[:, 0:1], out_gate[:, h, :],
                                                  ALU.mult, ALU.mult))
                    dve.wait_ge(S("o_spread"), h + 1)
                    dve.tensor_tensor(halves(oT[:, h, :]), halves(oT[:, h, :]), bank_pair((2, 4, 6, 2)[h]),
                                      ALU.mult).then_inc(S("o_scaled"), 1)
                dve.wait_ge(S("o_scaled"), HB)

            def prompt_attention():
                def scaled(n):
                    width = P * (1 + n // HA)
                    st = 4 * (n % 2)
                    dve.wait_ge(S("pp_exp"), n + 1)
                    link(dve.reciprocal(stat[:, st + 3:st + 4], stat[:, st + 2:st + 3]))
                    dve.tensor_scalar(prob_p[:, n % 2, :width], prob_p[:, n % 2, :width], stat[:, st + 3:st + 4], None,
                                      ALU.mult).then_inc(S("pp_done"), 1)

                def collect(n):
                    if n % 2:
                        t, hp = 1 + n // HA, n % HA // 2
                        dve.wait_ge(S("pv_done"), n + 1)
                        dve.tensor_copy(aT[:, hp, cols(t)], ps[:, 4 + hp % 2, 0:P]).then_inc(S("pa_out"), 1)

                for n in range(4 * HA):
                    width = P * (1 + n // HA)
                    st = 4 * (n % 2)
                    dve.wait_ge(S("pp_dots"), n + 1)
                    if n >= 2:
                        dve.wait_ge(S("pp_done"), n - 1)
                    link(dve.tensor_reduce(stat[:, st:st + 1], ps[:, n % 2, :width], AX_X, ALU.max))
                    dve.tensor_scalar(stat[:, st + 1:st + 2], stat[:, st:st + 1], -DH ** -0.5, None,
                                      ALU.mult).then_inc(S("pp_max"), 1)
                    if n:
                        scaled(n - 1)
                    if n >= 3:
                        collect(n - 3)
                    take_half()
                scaled(4 * HA - 1)
                for n in range(4 * HA - 3, 4 * HA):
                    collect(n)

            def sample_attention():
                dve.wait_ge(S("pa_out"), 16)
                dve.wait_ge(S("state_s_out"), 16 * HB)
                link(dve.memset(q_blk[:, :, :, :, :], 0.0))
                for hh in range(2):
                    for par in range(2):
                        at = par * 16 + hh * NQ
                        for pair in range(4):
                            b = 2 * pair + par
                            ins = dve.tensor_copy(q_blk[64 * hh:64 * hh + 64, pair, :, par, at:at + NQ],
                                                  qT[64 * hh:64 * hh + 64, :, NQ * b:NQ * b + NQ])
                ins.then_inc(S("q_blk_done"), 1)
                for pair in range(4):
                    for n in range(1, 32, 2):
                        m = 32 * pair + n
                        dve.wait_ge(S("kp_turned"), m + 1)
                        if m >= 3:
                            dve.wait_ge(S("kp_used"), m - 2)
                        dve.tensor_copy(kpT[:, m % 3, :], ps[:, KP_BANK[m % 3], :]).then_inc(S("kpT_odd"), 1)
                    dve.wait_ge(S("sp_dots"), pair + 1)
                    dve.tensor_reduce(stat[:, 12:13], flat[:, 0:PAST], AX_X, ALU.max)
                    link(dve.tensor_reduce(stat[:, 13:14], ps[:, 6, 0:NS], AX_X, ALU.max))
                    link(dve.tensor_tensor(stat[:, 8:9], stat[:, 12:13], stat[:, 13:14], ALU.max))
                    dve.tensor_scalar(stat[:, 9:10], stat[:, 8:9], -DH ** -0.5, None, ALU.mult).then_inc(S("sp_max"), 1)
                    dve.wait_ge(S("sp_exp"), pair + 1)
                    link(dve.tensor_tensor(stat[:, 14:15], stat[:, 10:11], stat[:, 11:12], ALU.add))
                    link(dve.reciprocal(stat[:, 15:16], stat[:, 14:15]))
                    dve.wait_ge(S("spn_turned"), pair + 1)
                    dve.tensor_copy(probT_new[:, :], ps[0:NS, 6, 0:P]).then_inc(S("spnT_done"), 1)
                    dve.wait_ge(S("v_used"), 2 * NPG * (pair + 1))
                    dve.tensor_scalar(o_rows[:, :, :], ps[:, 7, 0:2 * P].rearrange("p (r n) -> p r n", r=2),
                                      stat[:, 15:16], None, ALU.mult).then_inc(S("o_rows_done"), 1)
                    dve.wait_ge(S("o_rows_turned"), pair + 1)
                    for hh in range(2):
                        for par in range(2):
                            at = par * 16 + hh * NQ
                            b = 2 * pair + par
                            ins = dve.tensor_copy(
                                aT[64 * hh:64 * hh + 64, :, NQ * b:NQ * b + NQ],
                                ps[64 * hh:64 * hh + 64, 6, par * P:(par + 1) * P]
                                .rearrange("p (c r) -> p c r", c=4)[:, :, at:at + NQ])
                    ins.then_inc(S("aT_done"), 1)
                dve.wait_ge(S("aT_done"), 4)

            def projections():
                n = 0
                for x, hi, lo in ((aT, a_hi, a_lo), (oT, o_hi, o_lo)):
                    for c in range(4):
                        link(dve.tensor_copy(hi[:, c, :], x[:, c, :]))
                        dve.tensor_tensor(lo[:, c, :], x[:, c, :], hi[:, c, :].bitcast(F32),
                                          ALU.subtract).then_inc(S("mix_split"), 1)
                dve.wait_ge(S("mix_split"), 8)
                for c in range(DC):
                    g, a = c // 2, c % 2
                    dve.wait_ge(S("ga_done"), g + 1)
                    dve.wait_ge(S("gb_done"), g + 1)
                    if a == 0:
                        dve.wait_ge(S("proj_half"), g + 1)
                    else:
                        dve.wait_ge(S("unit_done"), at_unit["proj", g] + 1)
                    if c:
                        dve.wait_ge(S("merged"), c)
                    dve.tensor_tensor(halves(part_a[:, :]), halves(gate_a[:, a, :]), bank_pair(4 * a), ALU.mult)
                    link(dve.tensor_tensor(halves(part_b[:, :]), halves(gate_b[:, a, :]), bank_pair(4 * a + 2), ALU.mult))
                    link(dve.tensor_tensor(part_a[:, :], part_a[:, :], part_b[:, :], ALU.add))
                    link(dve.tensor_copy(m_hi[:, c, :], part_a[:, :]))
                    dve.tensor_tensor(m_lo[:, c, :], part_a[:, :], m_hi[:, c, :].bitcast(F32),
                                      ALU.subtract).then_inc(S("merged"), 1)
                dve.wait_ge(S("x_back"), 16)
                for c in range(DC):
                    g, a = c // 2, c % 2
                    if a == 0:
                        dve.wait_ge(S("out_half"), g + 1)
                    else:
                        dve.wait_ge(S("unit_done"), at_unit["out", g] + 1)
                    dve.tensor_tensor(halves(xT[:, c, :]), halves(xT[:, c, :]), bank_pair(4 * (g % 2) + 2 * a),
                                      ALU.add).then_inc(S("x_version"), 1)
                    sq_add(2, c)

            dve.wait_ge(S("cst_in"), 16)
            dve.tensor_copy(rows_b[:, :], cst[0:NS, C_ROWS:C_ROWS + 4 * P])
            dve.tensor_copy(ident_b[:, :], ident).then_inc(S("bf16_in"), 1)
            x_in()
            norm(0)
            dve.tensor_tensor(bound[:, 1, :], lbs[:, 1, :], lbs[:, 0, :], ALU.subtract)
            dve.tensor_tensor(bound[:, 0, :], lbs[:, 0, :], lbs[:, 1, :], ALU.subtract).then_inc(S("bound_in"), 1)
            ffn(1, 0, X_READ, 1)
            norm(1)
            token_major()
            dve.wait_ge(S("bound_done"), 1)
            for g in range(2):
                take(3 + 5 * g)
                features(g)
                head(2 * g)
                head(2 * g + 1)
            output_norm()
            biases()
            prompt_attention()
            sample_biases()
            sample_attention()
            projections()
            norm(2)
            ffn(2, 2 * HALF, X_OUT, None)
            for c in range(DC):
                dve.wait_ge(S("y_turned"), c + 1)
                dve.tensor_copy(yout[:, 1:NT, c * P:(c + 1) * P],
                                ps[:, 2 * (c % 4), :].rearrange("p (t n) -> p t n", t=4)).then_inc(S("y_out_p"), 1)

        @block.tensor
        def _(pe):
            def unit(u):
                pe.wait_ge(S("w_hi_done"), u + 1)
                pe.wait_ge(S("w_lo_done"), u + 1)
                return w_hi[:, u % NW, :], w_lo[:, u % NW, :]

            def product(dst, hi, lo, x_hi, x_lo, first, last):
                pe.matmul(dst, hi, x_lo, start=first, stop=False)
                pe.matmul(dst, lo, x_hi, start=False, stop=False)
                return pe.matmul(dst, hi, x_hi, start=False, stop=last)

            def x_in():
                pe.wait_ge(S("x_in"), 32)
                pe.wait_ge(S("cst_in"), 16)
                for c in range(DC):
                    if c >= 4:
                        pe.wait_ge(S("x_version"), c - 3)
                    for t in range(NT):
                        dst = ps[:, 2 * (c % 4) + 1, 0:NS] if t == 0 else ps[:, 2 * (c % 4), P * (t - 1):P * t]
                        ins = pe.transpose(dst, xin[0:rows(t), t, c * P:(c + 1) * P], ident[0:rows(t), 0:rows(t)])
                    ins.then_inc(S("x_turned"), 1)

            def norm(k):
                pe.wait_ge(S("sq_added"), DC * (k + 1))
                if k == 0:
                    pe.wait_ge(S("x_version"), DC)
                for h in range(2):
                    ins = pe.matmul(ps[:, h, 0:HT], ones, sqsum[:, h * HT:(h + 1) * HT], start=True, stop=True)
                ins.then_inc(S("ss_done"), 1)

            def ffn(f, G0, x0):
                for h in range(2):
                    for j in range(HALF):
                        G = G0 + h * HALF + j
                        u = at_unit[f"gu{f}", h * HALF + j]
                        hi, lo = unit(u)
                        if j >= 2:
                            pe.wait_ge(S("hid_done"), G - 1)
                        elif h == 1:
                            pe.wait_ge(S("x_version"), x0 + (6 if j == 0 else 8))
                        else:
                            pe.wait_ge(S("rms_done"), 2 * f - 1)
                        for k in range(DC):
                            if G == G0:
                                pe.wait_ge(S("n_done"), DC * (0 if f == 1 else 2) + k + 1)
                            for m in range(2):
                                at = (m * DC + k) * P
                                for t in range(2):
                                    ins = product(ps[:, 4 * (j % 2) + 2 * m + t, 0:HT], hi[:, at:at + P], lo[:, at:at + P],
                                                  n_hi[:, k, t * HT:(t + 1) * HT], n_lo[:, k, t * HT:(t + 1) * HT],
                                                  k == 0, k == DC - 1)
                        ins.then_inc(S("unit_done"), 1)
                    for c in range(DC):
                        u = at_unit[f"down{f}", h * DC + c]
                        hi, lo = unit(u)
                        if c < 2:
                            pe.wait_ge(S("hid_done"), G0 + (h + 1) * HALF - 1)
                        elif c < 4:
                            pe.wait_ge(S("hid_done"), G0 + (h + 1) * HALF)
                        else:
                            pe.wait_ge(S("x_version"), x0 + h * DC + min(c - 1, 4))
                        for k in range(HALF):
                            if k == HALF - 1:
                                pe.wait_ge(S("hid_done"), G0 + (h + 1) * HALF)
                            for t in range(2):
                                ins = product(ps[:, DOWN_BANK[c] + t, 0:HT], hi[:, k * P:(k + 1) * P], lo[:, k * P:(k + 1) * P],
                                              hid_hi[:, k, t * HT:(t + 1) * HT], hid_lo[:, k, t * HT:(t + 1) * HT],
                                              k == 0, k == HALF - 1)
                        ins.then_inc(S("unit_done"), 1)

            def tokens_unit(i, u, n, base):
                hi, lo = unit(u)
                for t in range(NT):
                    for k in range(DC):
                        if i == 0 and t == 0:
                            pe.wait_ge(S("n_done"), DC + k + 1)
                        at = slice(TILE_AT[t], TILE_AT[t] + P)
                        ins = product(flat[:, base + 256 * t:base + 256 * t + n], n_hi[:, k, at], n_lo[:, k, at],
                                      hi[:, k * n:(k + 1) * n], lo[:, k * n:(k + 1) * n], k == 0, k == DC - 1)
                ins.then_inc(S("unit_done"), 1)

            def turn(i):
                for m in TURNS_OF[i] if i >= 0 else []:
                    n, _, part = TURNS[m]
                    pe.wait_ge(S("tok_done"), i + 1)
                    if m:
                        pe.wait_ge(S("turned_out"), m)
                    for t in range(NT):
                        dst = ps[0:n, 7, 0:NS] if t == 0 else ps[0:n, 6, P * (t - 1):P * t]
                        ins = pe.transpose(dst, stage[0:rows(t), i % 2, t, part], ident[0:rows(t), 0:rows(t)])
                    ins.then_inc(S("turned"), 1)

            def token_major():
                for i in range(NTOK):
                    if i < 2:
                        pe.wait_ge(S("rms_done"), 2)
                        pe.wait_ge(S("x_version"), X_FFN1)
                    else:
                        pe.wait_ge(S("stage_done"), i - 1)
                    if i == 4:
                        pe.wait_ge(S("scored"), 4)
                    if i == 5:
                        pe.wait_ge(S("p_rel"), 12)
                    tokens_unit(i, at_unit["tok", i], TOKEN_COLS[i][1], 1536 * (i % 2))
                    turn(i - 1)
                    if i == 3:
                        index()

            def index():
                pe.wait_ge(S("stage_done"), 4)
                pe.wait_ge(S("turned_out"), len(TURNS_OF[0] + TURNS_OF[1] + TURNS_OF[2]))
                pe.wait_ge(S("picked"), 1)
                for g in range(2):
                    ins = pe.transpose(ps[:, 6, g * NS:(g + 1) * NS], pick[:, g, :], ident[0:NS, 0:NS])
                ins.then_inc(S("pick_turned"), 1)

                def keys(n):
                    kc, b = n // NB, n % NB
                    if b == 0:
                        pe.wait_ge(S(f"ip_in{kc % 2}"), 16 * 4 * NB * (kc // 2 + 1))
                    if n >= 2:
                        pe.wait_ge(S("ip_odd" if n % 2 else "ip_even"), n // 2)
                    for j in range(4):
                        ins = pe.transpose(ps[0:DI, n % 2, j * P:(j + 1) * P], ipage[:, kc % 3, 4 * b + j, :], ident)
                    ins.then_inc(S("ip_turned"), 1)

                def dots(n):
                    b, half = n % NB, n // 4
                    pe.wait_ge(S("ip_odd" if n % 2 else "ip_even"), n // 2 + 1)
                    if n % 4 == 0 and half >= 2:
                        pe.wait_ge(S("rel_done"), half - 1)
                    pe.matmul(ps[32 * (b % 4):32 * (b % 4) + 32, 4 + half % 2, :], iq_s[:, b, :],
                              ipT[:, n % 4, :], start=True, stop=True).then_inc(S("dots_done"), 1)

                def weighing(half):
                    kc = half // 2
                    if half == 0:
                        pe.wait_ge(S("weigh_done"), 1)
                    pe.wait_ge(S("rel_done"), half + 1)
                    if half % 2 == 0 and kc >= 2:
                        pe.wait_ge(S("scored"), kc - 1)
                    pe.matmul(ps[0:NS, 2 + kc % 2, :], weigh[:, half % 2, :], rel[:, half % 2, :],
                              start=half % 2 == 0, stop=half % 2 == 1).then_inc(S("weighed"), 1)

                keys(0)
                for n in range(GROUPS):
                    if n + 1 < GROUPS:
                        keys(n + 1)
                    dots(n)
                    if n % 4 == 1 and n >= 4:
                        weighing(n // 4 - 1)
                weighing(GROUPS // 4 - 1)
                for b in range(NB):
                    ins = pe.matmul(ps[32 * (b % 4):32 * (b % 4) + 32, 7, NS * (b // 4):NS * (b // 4 + 1)],
                                    iq_s[:, b, :], ikT[:, 0:NS], start=True, stop=True)
                ins.then_inc(S("new_dots"), 1)
                pe.wait_ge(S("rel_new"), 1)
                for g in range(2):
                    ins = pe.matmul(ps[0:NS, 6, 128:128 + NS], weigh[:, g, :], rel[:, 0, g * NS:(g + 1) * NS],
                                    start=g == 0, stop=g == 1)
                ins.then_inc(S("new_weighed"), 1)
                for m in range(12):
                    t, h = 2 + m // 4, m % 4
                    if m >= 2:
                        pe.wait_ge(S("p_rel"), m - 1)
                    pe.matmul(ps[:, 4 + m % 2, 0:P * t], iqT[:, h, cols(t)], ikT[:, NS:NS + P * t],
                              start=True, stop=True).then_inc(S("p_dots"), 1)

            def features(g):
                i = NTOK + g
                if g == 0:
                    pe.wait_ge(S("turned_out"), len(TURNS))
                    pe.wait_ge(S("stage_done"), NTOK)
                else:
                    pe.wait_ge(S("state_s_done"), 2)
                tokens_unit(i, at_unit["tok", i], 256, 2560)
                for r in range(3):
                    u = at_unit["feat", 3 * g + r]
                    hi, lo = unit(u)
                    if r == 0 and g:
                        pe.wait_ge(S("o_out"), 2)
                    if r == 1:
                        pe.wait_ge(S("stage_done"), i + 1)
                    if r == 2:
                        pe.wait_ge(S("feat_done"), 6 * g + 2)
                    for a in range(2):
                        for k in range(DC):
                            at = k * 256 + a * P
                            for t in range(2):
                                ins = product(ps[:, 4 * (r % 2) + 2 * a + t, 0:HT], hi[:, at:at + P], lo[:, at:at + P],
                                              n_hi[:, k, t * HT:(t + 1) * HT], n_lo[:, k, t * HT:(t + 1) * HT],
                                              k == 0, k == DC - 1)
                    ins.then_inc(S("unit_done"), 1)

            def head(h):
                a, g = h % 2, h // 2
                if a == 0:
                    pe.wait_ge(S("feat_ready"), g + 1)
                    pe.wait_ge(S("feat_done"), 6 * g + 6)
                else:
                    pe.wait_ge(S("state_s_done"), h)
                for L in range(len(LEVELS)):
                    if L:
                        pe.wait_ge(S("level_in"), 8 * h + L)
                    if L >= 2:
                        pe.wait_ge(S("level_out"), 8 * h + L - 1)
                    q = q_lev[:, L % 2, :] if L else query[:, a, :]
                    k = k_lev[:, L % 2, :] if L else key[:, a, :]
                    if LEVELS[L] < NQ:
                        pe.matmul(ps[0:NS, 6 + L % 2, 0:NS], k[:, 0:NS], q[:, 0:NS], start=True, stop=True)
                    for t in range(1, NT):
                        ins = pe.matmul(ps[:, 4 + L % 2, P * (t - 1):P * t], k[:, cols(t)], q[:, cols(t)],
                                        start=True, stop=True)
                    ins.then_inc(S("level_done"), 1)
                pe.wait_ge(S("level_in"), 8 * h + 8)
                pe.wait_ge(S("level_out"), 8 * h + 8)
                for t in range(NT):
                    dst = ps[0:NS, 6, 0:KD] if t == 0 else ps[:, 4, P * (t - 1):P * t]
                    ins = pe.transpose(dst, k_lev[:, 0, cols(t)], ident)
                ins.then_inc(S("k_turned"), 1)
                pe.wait_ge(S("k_rows_done"), h + 1)
                if h:
                    pe.wait_ge(S("o_out"), h)
                v = [stage[0:rows(t), g, t, a * VD:(a + 1) * VD] for t in range(NT)]
                for i in range(4):
                    if i >= 2:
                        pe.wait_ge(S("state_done"), 4 * h + i - 1)
                    pe.matmul(ps[:, 2 + i % 2, 0:VD], k_rows[:, i + 1, :], v[i + 1], start=True,
                              stop=True).then_inc(S("state_added"), 1)
                    pe.matmul(ps[:, 0, P * i:P * i + P], v[i + 1], att[:, i, :], start=True, stop=i == 0)
                    if i:
                        pe.wait_ge(S("state_done"), 4 * h + i)
                        pe.matmul(ps[:, 0, P * i:P * i + P], state[:, (i + 1) % 2, :], q_lev[:, 0, cols(i + 1)],
                                  start=False, stop=True).then_inc(S("state_used"), 1)
                pe.wait_ge(S("state_in"), 16 * (h + 1))
                pe.matmul(ps[:, 1, 0:NS], v[0], att_s[:, :], start=True, stop=False)
                for b in range(NB):
                    ins = pe.matmul(ps[:, 1, NQ * b:NQ * b + NQ], state_s[:, b, :], q_lev[:, 0, NQ * b:NQ * b + NQ],
                                    start=False, stop=b == NB - 1)
                ins.then_inc(S("o_summed"), 1)
                pe.wait_ge(S("v_own_done"), h + 1)
                for m in range(2):
                    ins = pe.matmul(ps[:, 5 + 2 * m, :], k_rows[0:NS, 0, :],
                                    v_own[:, 4 * m:4 * m + 4, :], start=True, stop=True)
                ins.then_inc(S("head_read"), 1)

            def output_norm():
                for h in range(HB):
                    pe.wait_ge(S("o_sq_done"), h + 1)
                    for t in range(2):
                        ins = pe.matmul(ps[32 * h:32 * h + 32, t, 0:HT], ones[:, 0:32],
                                        o_sq[:, h % 2, t * HT:(t + 1) * HT], start=True, stop=True)
                    ins.then_inc(S("o_sq_used"), 1)
                pe.wait_ge(S("o_inv_done"), 1)
                pe.wait_ge(S("state_s_done"), HB)
                for h in range(HB):
                    if h == 3:
                        pe.wait_ge(S("o_scaled"), 1)
                    for t in range(2):
                        ins = pe.matmul(ps[:, (2, 4, 6, 2)[h] + t, 0:HT], ones[32 * h:32 * h + 1, :],
                                        o_rms[32 * h:32 * h + 1, t * HT:(t + 1) * HT], start=True, stop=True)
                    ins.then_inc(S("o_spread"), 1)

            def prompt_attention():
                def dots(n):
                    t, h = 1 + n // HA, n % HA
                    width, at, part = P * t, P * t * (t - 1) // 2, slice(64 * (h % 2), 64 * (h % 2) + 64)
                    if n >= 2:
                        pe.wait_ge(S("pp_exp"), n - 1)
                    pe.matmul(ps[:, n % 2, :width], ident_b[:, :], bias_p[:, at:at + width], start=True, stop=False)
                    pe.matmul(ps[:, n % 2, :width], qT[part, h // 2, cols(t)], kT[part, h // 2, NS:NS + width],
                              start=False, stop=True).then_inc(S("pp_dots"), 1)

                def turn(n):
                    t = 1 + n // HA
                    pe.wait_ge(S("pp_done"), n + 1)
                    if n >= 2:
                        pe.wait_ge(S("ppT_done"), n - 1)
                    for s in range(t):
                        ins = pe.transpose(ps[:, 2 + n % 2, s * P:(s + 1) * P], prob_p[:, n % 2, s * P:(s + 1) * P], ident)
                    ins.then_inc(S("pp_turned"), 1)

                def values(n):
                    t, h = 1 + n // HA, n % HA
                    pe.wait_ge(S("ppT_done"), n + 1)
                    if n >= 4 and n % 2 == 0:
                        pe.wait_ge(S("pa_out"), n // 2 - 1)
                    for s in range(t):
                        ins = pe.matmul(ps[64 * (h % 2):64 * (h % 2) + 64, 4 + h // 2 % 2, 0:P],
                                        v_tok[:, s, DH * h:DH * (h + 1)], probT_p[:, n % 2, s, :],
                                        start=s == 0, stop=s == t - 1)
                    ins.then_inc(S("pv_done"), 1)

                pe.wait_ge(S("prompt_biased"), 1)
                pe.wait_ge(S("v_back"), 16)
                dots(0)
                for n in range(4 * HA):
                    if n + 1 < 4 * HA:
                        dots(n + 1)
                    if n:
                        values(n - 1)
                    turn(n)
                values(4 * HA - 1)

            def sample_attention():
                pe.wait_ge(S("q_blk_done"), 1)
                pe.wait_ge(S("biased"), 1)
                pe.wait_ge(S("v_new_back"), 16)
                for pair in range(4):
                    if pair:
                        pe.wait_ge(S("sp_exp"), pair)
                        pe.wait_ge(S("aT_done"), pair)
                        pe.wait_ge(S("spT_done"), 4 * pair)
                    pick_rows = rows_b[:, pair * P:(pair + 1) * P]
                    pe.matmul(ps[:, 6, 0:NS], pick_rows, bias_s[:, PAST:], start=True, stop=False,
                              skip_group_check=True)
                    for hp in range(4):
                        for par in range(2):
                            pe.matmul(ps[32 * hp:32 * hp + 32, 6, 0:NS], q_blk[:, pair, hp, par, :], kT[:, hp, 0:NS],
                                      start=False, stop=par == 1, skip_group_check=True)

                    def turn(n):
                        m, slot = 32 * pair + n, (8 * pair + n // 4) % K_RING
                        if n % 4 == 0:
                            pe.wait_ge(S(f"k_in{slot}"), 64 * ((8 * pair + n // 4) // K_RING + 1))
                        if m >= 3:
                            pe.wait_ge(S("kpT_even" if m % 2 else "kpT_odd"), (m - 3) // 2 + 1)
                        for j in range(4):
                            ins = pe.transpose(ps[:, KP_BANK[m % 3], j * P:(j + 1) * P],
                                               k_page[:, slot, j, P * (n % 4):P * (n % 4) + P], ident)
                        ins.then_inc(S("kp_turned"), 1)

                    turn(0)
                    turn(1)
                    for n in range(32):
                        kc, par, hp = n // 8, n // 4 % 2, n % 4
                        if n + 2 < 32:
                            turn(n + 2)
                        if n % 8 == 0:
                            pe.matmul(ps[:, kc, :], pick_rows, bias_s[:, 512 * kc:512 * kc + 512], start=True,
                                      stop=False, skip_group_check=True)
                        pe.wait_ge(S("kpT_odd" if n % 2 else "kpT_even"), (32 * pair + n) // 2 + 1)
                        ins = pe.matmul(ps[32 * hp:32 * hp + 32, kc, :], q_blk[:, pair, hp, par, :], kpT[:, (32 * pair + n) % 3, :],
                                        start=False, stop=par == 1, skip_group_check=True)
                        ins.then_inc(S("kp_used"), 1)
                    pe.wait_ge(S("kp_used"), 32 * pair + 32)
                    pe.sem_inc(S("sp_dots"), 1)
                    pe.wait_ge(S("sp_exp"), pair + 1)
                    pe.transpose(ps[0:NS, 6, 0:P], prob[:, PAST:], ident).then_inc(S("spn_turned"), 1)

                    def turn_probs(j):
                        if j >= 2:
                            pe.wait_ge(S("spT_done"), 4 * pair + j - 1)
                        for i in range(4):
                            at = (4 * j + i) * P
                            ins = pe.transpose(ps[:, 4 + j % 2, i * P:(i + 1) * P], prob[:, at:at + P], ident)
                        ins.then_inc(S("sp_turned"), 1)

                    turn_probs(0)
                    pe.wait_ge(S("spnT_done"), pair + 1)
                    for hp in range(4):
                        for par in range(2):
                            pe.matmul(ps[32 * hp:32 * hp + 32, 7, par * P:(par + 1) * P], probT_new[:, 32 * hp:32 * hp + 32],
                                      v_new[:, P * hp:P * hp + P], start=par == 0, stop=False, skip_group_check=True)
                    for j in range(4):
                        if j < 3:
                            turn_probs(j + 1)
                        pe.wait_ge(S("spT_done"), 4 * pair + j + 1)
                        for i in range(4):
                            for par in range(2):
                                m = 2 * NPG * pair + 2 * (4 * j + i) + par
                                pe.wait_ge(S(f"v_in{m % V_RING}"), 16 * (m // V_RING + 1))
                                for hp in range(4):
                                    ins = pe.matmul(ps[32 * hp:32 * hp + 32, 7, par * P:(par + 1) * P],
                                                    probT[:, j % 2, i, 32 * hp:32 * hp + 32],
                                                    v_page[:, m % V_RING, P * hp:P * hp + P], start=False,
                                                    stop=4 * j + i == NPG - 1, skip_group_check=True)
                                ins.then_inc(S("v_used"), 1)
                    pe.wait_ge(S("o_rows_done"), pair + 1)
                    for par in range(2):
                        ins = pe.transpose(ps[:, 6, par * P:(par + 1) * P], o_rows[:, par, :], ident)
                    ins.then_inc(S("o_rows_turned"), 1)

            def projections():
                def gate(name, g, bank):
                    hi, lo = unit(at_unit[name, g])
                    for a in range(2):
                        for k in range(DC):
                            at = k * 256 + a * P
                            for t in range(2):
                                ins = product(ps[:, bank + 2 * a + t, 0:HT], hi[:, at:at + P], lo[:, at:at + P],
                                              n_hi[:, k, t * HT:(t + 1) * HT], n_lo[:, k, t * HT:(t + 1) * HT],
                                              k == 0, k == DC - 1)
                    ins.then_inc(S("unit_done"), 1)

                for g in range(DC // 2):
                    if g == 0:
                        pe.wait_ge(S("aT_done"), 4)
                    else:
                        pe.wait_ge(S("merged"), 2 * g - 1)
                    gate("ga", g, 0)
                    if g:
                        pe.wait_ge(S("merged"), 2 * g)
                    gate("gb", g, 4)
                    hi, lo = unit(at_unit["proj", g])
                    if g == 0:
                        pe.wait_ge(S("mix_split"), 8)
                    for a in range(2):
                        pe.wait_ge(S("gb_done" if a else "ga_done"), g + 1)
                        for m, (x_hi, x_lo) in enumerate(((a_hi, a_lo), (o_hi, o_lo))):
                            for k in range(4):
                                at = (4 * m + k) * 256 + a * P
                                for t in range(2):
                                    ins = product(ps[:, 4 * a + 2 * m + t, 0:HT], hi[:, at:at + P], lo[:, at:at + P],
                                                  x_hi[:, k, t * HT:(t + 1) * HT], x_lo[:, k, t * HT:(t + 1) * HT],
                                                  k == 0, k == 3)
                        ins.then_inc(S("unit_done" if a else "proj_half"), 1)
                for g in range(DC // 2):
                    hi, lo = unit(at_unit["out", g])
                    for a in range(2):
                        if g == 0:
                            pe.wait_ge(S("merged"), DC - 1 if a == 0 else DC)
                        elif g >= 2:
                            pe.wait_ge(S("x_version"), X_FFN1 + 2 * (g - 2) + a + 1)
                        for k in range(DC):
                            if g == 0 and k == DC - 1:
                                pe.wait_ge(S("merged"), DC)
                            at = k * 256 + a * P
                            for t in range(2):
                                ins = product(ps[:, 4 * (g % 2) + 2 * a + t, 0:HT], hi[:, at:at + P], lo[:, at:at + P],
                                              m_hi[:, k, t * HT:(t + 1) * HT], m_lo[:, k, t * HT:(t + 1) * HT],
                                              k == 0, k == DC - 1)
                        ins.then_inc(S("unit_done" if a else "out_half"), 1)

            x_in()
            norm(0)
            ffn(1, 0, X_READ)
            norm(1)
            token_major()
            for g in range(2):
                features(g)
                head(2 * g)
                head(2 * g + 1)
            output_norm()
            prompt_attention()
            sample_attention()
            projections()
            norm(2)
            ffn(2, 2 * HALF, X_OUT)
            for c in range(DC):
                pe.wait_ge(S("x_version"), X_OUT + DC + DC if c < 4 else X_FFN2)
                if c >= 4:
                    pe.wait_ge(S("y_out_p"), c - 3)
                    pe.wait_ge(S("y_out_s"), c - 3)
                for t in range(NT):
                    dst = ps[0:NS, 2 * (c % 4) + 1, 0:P] if t == 0 else ps[:, 2 * (c % 4), P * (t - 1):P * t]
                    ins = pe.transpose(dst, xT[:, c, cols(t)], ident)
                ins.then_inc(S("y_turned"), 1)


_OUTS = [(1, SEQ, D), (NB, NQ, D), (1, 1, SEQ, HA, DH), (1, 1, SEQ, HA, DH), (1, 1, SEQ, DI), (1, 1, HB, KD, VD),
         (1, NB, NQ, HA, DH), (1, NB, NQ, HA, DH), (1, NB, NQ, DI), (1, NB, HB, KD, VD)]


def kernel(**inputs):
    import concourse.bacc as _bacc
    from concourse.bass_utils import run_bass_kernel_spmd as _run

    nc = _bacc.Bacc("TRN2", target_bir_lowering=False, num_devices=1)
    arrays, w, out = {}, {}, []
    drop = ("ffn1_w_gate", "ffn1_w_up", "ffn1_w_down", "w_in", "q_norm", "k_norm",
            "w_proj_attn", "w_proj_hgrn", "w_out", "ffn2_w_gate", "ffn2_w_up",
            "ffn2_w_down", "cache_k", "cache_v", "cache_idx_k", "state_hgrn")
    given = {name: np.ascontiguousarray(a) for name, a in inputs.items()}
    norms = [given.pop(name)[0] for name in ("ffn1_norm", "mix_norm", "ffn2_norm")]
    given["gains"] = np.ascontiguousarray(np.stack(norms).reshape(3, DC, P).transpose(2, 0, 1))
    given["lbs"] = np.ascontiguousarray(given.pop("hgrn_lb").reshape(2, HB, P).transpose(2, 0, 1))
    given["gain_o"] = given.pop("hgrn_o_norm").reshape(P, 1)
    given["cst"] = constants()
    given["lmask"] = level_masks()
    for name, a in given.items():
        a = a[0] if name in drop else a
        arrays[f"in_{name}"] = a
        w[name] = nc.dram_tensor(f"in_{name}", a.shape, mybir.dt.from_np(a.dtype), kind="ExternalInput").ap()
    for i, shape in enumerate(_OUTS):
        out.append(nc.dram_tensor(f"out_{i}", shape, F32, kind="ExternalOutput").ap())
    build(nc, w, out)
    r = _run(nc, [arrays], core_ids=[0])
    return tuple(r.results[0][f"out_{i}"] for i in range(len(_OUTS)))
```
